# Optimizing a Trainium2 kernel written in Bass

```python
import jax, jax.numpy as jnp
from jax import lax
import numpy as np

D_MODEL = 2048
BATCH = 1
SEQ = 256
DEPTH = 1

CHUNK = 64
D_MIX = D_MODEL
D_CONV = D_MIX // 2
CONV_K = 31
D_SSD = D_MIX - D_CONV
SSD_HEAD_DIM = 64
SSD_HEADS = D_SSD // SSD_HEAD_DIM
SSD_GROUPS = 4
SSD_STATE = 128
SSD_CONV_K = 4
D_XBC = D_SSD + 2 * SSD_GROUPS * SSD_STATE
D_IN = 2 * D_CONV + D_SSD + D_XBC + SSD_HEADS
D_FF = -(-(8 * D_MODEL) // (3 * 256)) * 256
EPS = 1e-6

kernel_name = "hybrid_conformer_conv_mamba2_ssd_block"

def rmsnorm(x, g):
    xf = x.astype(jnp.float32)
    y = xf * lax.rsqrt(jnp.mean(xf * xf, axis=-1, keepdims=True) + EPS)
    return (y * g.astype(jnp.float32)).astype(x.dtype)

def layernorm(x, g, b):
    xf = x.astype(jnp.float32)
    mu = jnp.mean(xf, axis=-1, keepdims=True)
    var = jnp.mean(jnp.square(xf - mu), axis=-1, keepdims=True)
    y = (xf - mu) * lax.rsqrt(var + EPS)
    return (y * g.astype(jnp.float32) + b.astype(jnp.float32)).astype(x.dtype)

def causal_depthwise_conv(u, w, b):
    k, c = w.shape
    out = lax.conv_general_dilated(
        u, w[:, None, :].astype(u.dtype), window_strides=(1,), padding=[(k - 1, 0)],
        dimension_numbers=("NWC", "WIO", "NWC"), feature_group_count=c)
    return out + b.astype(u.dtype)

def segsum(a):
    cs = jnp.cumsum(a, axis=-1)
    diff = cs[..., :, None] - cs[..., None, :]
    l = a.shape[-1]
    mask = jnp.tril(jnp.ones((l, l), dtype=bool))
    return jnp.where(mask, diff, -jnp.inf)

def ssd_chunked(xh, dt, a_head, bm, cm):
    bsz, s, h, p = xh.shape
    g, n = bm.shape[2], bm.shape[3]
    r = h // g
    nc = s // CHUNK
    xd = (xh * dt[..., None]).reshape(bsz, nc, CHUNK, g, r, p)
    a = (dt * a_head).reshape(bsz, nc, CHUNK, g, r).transpose(0, 3, 4, 1, 2)
    bc = bm.reshape(bsz, nc, CHUNK, g, n)
    cc = cm.reshape(bsz, nc, CHUNK, g, n)
    a_cs = jnp.cumsum(a, axis=-1)
    decay_mat = jnp.exp(segsum(a))
    scores = jnp.einsum("bclgn,bcsgn->bgcls", cc, bc)
    y_diag = jnp.einsum("bgrcls,bcsgrp->bclgrp", scores[:, :, None] * decay_mat, xd)
    decay_states = jnp.exp(a_cs[..., -1:] - a_cs)
    states = jnp.einsum("bclgn,bgrcl,bclgrp->bcgrpn", bc, decay_states, xd)
    chunk_decay = jnp.exp(a_cs[..., -1])

    def step(hstate, inp):
        st, dec = inp
        return hstate * dec[..., None, None] + st, hstate

    h0 = jnp.zeros((bsz, g, r, p, n), dtype=xd.dtype)
    _, prev = lax.scan(step, h0, (states.transpose(1, 0, 2, 3, 4, 5),
                                  chunk_decay.transpose(3, 0, 1, 2)))
    prev = prev.transpose(1, 0, 2, 3, 4, 5)
    y_off = jnp.einsum("bclgn,bcgrpn,bgrcl->bclgrp", cc, prev, jnp.exp(a_cs))
    return (y_diag + y_off).reshape(bsz, s, h, p)

def setup_inputs(seed: int = 0) -> dict:
    key = jax.random.key(seed)
    ks = jax.random.split(key, 24)
    f32 = jnp.float32

    def nrm(k, shape, scale):
        return jax.random.normal(k, shape, f32) * scale

    def gain(k, shape):
        return 1.0 + 0.05 * jax.random.normal(k, shape, f32)

    L = DEPTH
    x = jax.random.normal(ks[0], (BATCH, SEQ, D_MODEL), f32)
    norm_mix_pre = gain(ks[1], (L, D_MODEL))
    w_in = nrm(ks[2], (L, D_MODEL, D_IN), D_MODEL ** -0.5)
    conv_dw_w = nrm(ks[3], (L, CONV_K, D_CONV), CONV_K ** -0.5)
    conv_dw_b = nrm(ks[4], (L, D_CONV), 0.02)
    conv_ln_g = gain(ks[5], (L, D_CONV))
    conv_ln_b = nrm(ks[6], (L, D_CONV), 0.02)
    ssd_conv_w = nrm(ks[7], (L, SSD_CONV_K, D_XBC), SSD_CONV_K ** -0.5)
    ssd_conv_b = nrm(ks[8], (L, D_XBC), 0.02)
    dt0 = jnp.exp(jax.random.uniform(ks[9], (L, SSD_HEADS), f32,
                                     minval=np.log(1e-3), maxval=np.log(1e-1)))
    ssd_dt_bias = dt0 + jnp.log(-jnp.expm1(-dt0))
    ssd_a_log = jnp.log(jax.random.uniform(ks[10], (L, SSD_HEADS), f32, minval=1.0, maxval=16.0))
    ssd_d = gain(ks[11], (L, SSD_HEADS))
    ssd_norm_w = gain(ks[12], (L, D_SSD))
    w_out = nrm(ks[13], (L, D_MIX, D_MODEL), D_MIX ** -0.5)
    norm_mix_post = gain(ks[14], (L, D_MODEL))
    norm_ffn_pre = gain(ks[15], (L, D_MODEL))
    w_gate = nrm(ks[16], (L, D_MODEL, D_FF), D_MODEL ** -0.5)
    w_up = nrm(ks[17], (L, D_MODEL, D_FF), D_MODEL ** -0.5)
    w_down = nrm(ks[18], (L, D_FF, D_MODEL), D_FF ** -0.5)
    norm_ffn_post = gain(ks[19], (L, D_MODEL))
    return {"x": x, "norm_mix_pre": norm_mix_pre, "w_in": w_in,
            "conv_dw_w": conv_dw_w, "conv_dw_b": conv_dw_b,
            "conv_ln_g": conv_ln_g, "conv_ln_b": conv_ln_b,
            "ssd_conv_w": ssd_conv_w, "ssd_conv_b": ssd_conv_b,
            "ssd_dt_bias": ssd_dt_bias, "ssd_a_log": ssd_a_log, "ssd_d": ssd_d,
            "ssd_norm_w": ssd_norm_w, "w_out": w_out, "norm_mix_post": norm_mix_post,
            "norm_ffn_pre": norm_ffn_pre, "w_gate": w_gate, "w_up": w_up,
            "w_down": w_down, "norm_ffn_post": norm_ffn_post}

def reference(x, norm_mix_pre, w_in, conv_dw_w, conv_dw_b, conv_ln_g, conv_ln_b,
              ssd_conv_w, ssd_conv_b, ssd_dt_bias, ssd_a_log, ssd_d, ssd_norm_w,
              w_out, norm_mix_post, norm_ffn_pre, w_gate, w_up, w_down, norm_ffn_post):
    bsz, s, _ = x.shape
    f32 = jnp.float32
    for l in range(DEPTH):
        h = rmsnorm(x, norm_mix_pre[l])
        proj = h @ w_in[l]
        c_a, c_g, z, xbc, dt_raw = jnp.split(
            proj, [D_CONV, 2 * D_CONV, 2 * D_CONV + D_SSD, 2 * D_CONV + D_SSD + D_XBC], axis=-1)

        u = c_a * jax.nn.sigmoid(c_g)
        u = causal_depthwise_conv(u, conv_dw_w[l], conv_dw_b[l])
        u = jax.nn.silu(layernorm(u, conv_ln_g[l], conv_ln_b[l]))

        xbc = jax.nn.silu(causal_depthwise_conv(xbc, ssd_conv_w[l], ssd_conv_b[l]))
        xs, bm, cm = jnp.split(xbc, [D_SSD, D_SSD + SSD_GROUPS * SSD_STATE], axis=-1)
        xh = xs.astype(f32).reshape(bsz, s, SSD_HEADS, SSD_HEAD_DIM)
        bm = bm.astype(f32).reshape(bsz, s, SSD_GROUPS, SSD_STATE)
        cm = cm.astype(f32).reshape(bsz, s, SSD_GROUPS, SSD_STATE)
        dt = jax.nn.softplus(dt_raw.astype(f32) + ssd_dt_bias[l].astype(f32))
        a_head = -jnp.exp(ssd_a_log[l].astype(f32))
        y = ssd_chunked(xh, dt, a_head, bm, cm)
        y = y + xh * ssd_d[l].astype(f32)[:, None]
        y = y.reshape(bsz, s, D_SSD) * jax.nn.silu(z.astype(f32))
        yg = y.reshape(bsz, s, SSD_GROUPS, D_SSD // SSD_GROUPS)
        yg = yg * lax.rsqrt(jnp.mean(yg * yg, axis=-1, keepdims=True) + EPS)
        y = (yg.reshape(bsz, s, D_SSD) * ssd_norm_w[l].astype(f32)).astype(x.dtype)

        mix = jnp.concatenate([u, y], axis=-1) @ w_out[l]
        x = x + rmsnorm(mix, norm_mix_post[l])

        h = rmsnorm(x, norm_ffn_pre[l])
        f = (jax.nn.silu(h @ w_gate[l]) * (h @ w_up[l])) @ w_down[l]
        x = x + rmsnorm(f, norm_ffn_post[l])
    return x


_drawn_inputs = setup_inputs


def setup_inputs(seed=0):
    import zlib

    import numpy as np

    out = dict(_drawn_inputs(seed))
    spreads = {}
    factors = {'conv_dw_b': 3.055, 'conv_ln_b': 6.401, 'ssd_conv_b': 2.939}
    for name, (base, spread) in spreads.items():
        noise = np.random.default_rng([zlib.crc32(name.encode()), seed]).standard_normal(out[name].shape)
        drawn = base * np.exp(spread * noise) if base else spread * noise
        out[name] = __import__('jax').numpy.asarray(drawn.astype(out[name].dtype))
    for name, factor in factors.items():
        out[name] = (out[name] * factor).astype(out[name].dtype)
    return out
```

```python
from contextlib import ExitStack

import concourse.bass as bass
from concourse import mybir

F32 = mybir.dt.float32
F32R = mybir.dt.float32r
ACT = mybir.ActivationFunctionType
ALU = mybir.AluOpType

P = 128
T = 256
TH = T // P
D = 2048
KC = D // P
DC = 1024
DS = 1024
CB, SB = DC // P, DS // P
TAPS = 31
TAPS4 = 4
HEADS = 16
HD = 64
GROUPS = 4
HPG = HEADS // GROUPS
FF = 5632
FC = FF // P
EPS = 1e-6
SLOTS = 4
UNIT = 1024
SLAB = 256
MAIN, CROSS = slice(0, T), slice(T, 2 * T)

COL_A, COL_GATE, COL_Z, COL_XBC, COL_DT = 0, DC, 2 * DC, 2 * DC + DS, 2 * DC + DS + 2048
PAIRS = DC // SLAB
XBC_SLABS = 2048 // SLAB
Z_SLABS = DS // SLAB
SLAB_X = 2 * PAIRS
SLAB_Z = SLAB_X + XBC_SLABS
SLAB_FFN = SLAB_Z + Z_SLABS
FFN_PAIRS = FF // SLAB
QUAD_WOUT = SLAB_FFN
QUAD_FFN = QUAD_WOUT + D * D // (P * UNIT * 4)
QUAD_DOWN = QUAD_FFN + 2 * FFN_PAIRS
FFN_OFF = 4 * (QUAD_FFN - SLAB_FFN) + 4
DOWN_UNITS = FC // 2
NCH = D // 512
BANK_CREDIT = 3

PCOLS = [("mix_g", KC), ("ffn_g", KC), ("dw_w", CB * TAPS), ("dw_b", CB), ("ln_g", CB), ("ln_b", CB),
         ("xw", 16 * TAPS4), ("xb", 16), ("d_skip", SB), ("gn_w", SB), ("dt_bias", HEADS), ("a_log", HEADS)]
PAT, _n = {}, 0
for _name, _w in PCOLS:
    PAT[_name] = _n
    _n += _w
NPAR = _n

SERIES = [1.0 / (2 * i + 1) for i in range(9)]


def build(nc, x, w_in, w_out, w_gate, w_up, w_down, params, post_mix, post_ffn, out):
    ctx = ExitStack()
    with ctx:
        place = {"at": nc.sbuf_base}

        def sb(name, shape, dt=F32, at=None):
            size = 4
            for n in shape[1:]:
                size *= n
            size = -(-size // 32) * 32
            here = place["at"] if at is None else at
            if at is None:
                place["at"] += size
            return nc.alloc_sbuf_tensor_at(name, shape, dt, offset=here), here + size

        def keep(name, shape, dt=F32):
            return sb(name, shape, dt)[0]

        def sem(name):
            return ctx.enter_context(nc.semaphore(name))

        place["at"] = -(-place["at"] // 64) * 64
        raw = keep("raw", [P, SLOTS, UNIT])
        w_hi = keep("w_hi", [P, SLOTS, UNIT], F32R)
        w_lo = keep("w_lo", [P, SLOTS, UNIT], F32R)
        x_row = keep("x_row", [P, TH, D])
        acts_at = place["at"]
        acts = keep("acts", [P, KC, 2, T], F32R)
        post_g = keep("post_g", [P, D])
        par = keep("par", [P, NPAR])
        ident = keep("ident", [P, P])
        mean_w = keep("mean_w", [P, P])
        cross = keep("cross", [P, 2, 2, T])
        g_sum = keep("g_sum", [P, 2, T])
        u_sum = keep("u_sum", [P, 2, T])
        stat = keep("stat", [P, 48])
        phase = place["at"]
        hidden, end_ffn = sb("hidden", [P, FC, 2, T], F32R, phase)
        f_row, _ = sb("f_row", [P, TH, D], F32, acts_at)
        xbc, e = sb("xbc", [P, 16, T], F32, phase)
        row_work, _ = sb("row_work", [P, TH, D], F32, phase)
        PADW = T + TAPS - 1
        upad, e = sb("upad", [P, CB, PADW], F32, e)
        u, e = sb("u", [P, CB, T], F32, e)
        XPW = T + TAPS4 - 1
        xpad, e = sb("xpad", [P, 2, 2, XPW], F32, e)
        z, e = sb("z", [P, SB, T], F32, e)
        xd, e = sb("xd", [P, TH, DS], F32, e)
        mask, e = sb("mask", [P, T + P], F32, e)
        scores, e = sb("scores", [P, GROUPS, T + P], F32, e)
        decay, e = sb("decay", [P, 2, HPG, T + P], F32, e)
        sel, e = sb("sel", [HEADS, HEADS, P], F32, e)
        cs_row, e = sb("cs_row", [HEADS, T], F32, e)
        dt_raw, e = sb("dt_raw", [P, KC, HEADS], F32, e)
        dt_hi, e = sb("dt_hi", [P, KC, HEADS], F32R, e)
        dt_lo, e = sb("dt_lo", [P, KC, HEADS], F32R, e)
        sm, e = sb("sm", [P, 12, 2 * HEADS], F32, e)
        assert max(e, end_ffn) <= nc.sbuf_usable_end, (e, end_ffn, nc.sbuf_usable_end)

        ps = ctx.enter_context(nc.psum_tensor("ps", [P, 8, 512], F32))

        unit_loaded = [sem(f"unit_loaded{i}") for i in range(SLOTS)]
        x_loaded = [sem(f"x_loaded{i}") for i in range(TH)]
        par_loaded = sem("par_loaded")
        dtw_loaded = sem("dtw_loaded")
        postg_loaded = sem("postg_loaded")
        consts = sem("consts")
        hi_made = sem("hi_made")
        lo_made = sem("lo_made")
        multiplied = sem("multiplied")
        slab_done = sem("slab_done")
        crossed = sem("crossed")
        summed = sem("summed")
        row_sq = sem("row_sq")
        row_rms = sem("row_rms")
        row_rstd = sem("row_rstd")
        row_scaled = sem("row_scaled")
        turned = sem("turned")
        norm_hi = sem("norm_hi")
        norm_lo = sem("norm_lo")
        dt_done = sem("dt_done")
        dts = sem("dts")
        dte = sem("dte")
        dtw_hi_made = sem("dtw_hi_made")
        dtw_lo_made = sem("dtw_lo_made")
        a_ready = sem("a_ready")
        cs_done = sem("cs_done")
        cs_copied = sem("cs_copied")
        csT_done = sem("csT_done")
        csT_copied = sem("csT_copied")
        gate_sig = sem("gate_sig")
        glu_done = sem("glu_done")
        conv_tap = sem("conv_tap")
        xtap = sem("xtap")
        x_act = sem("x_act")
        z_act = sem("z_act")
        xs_turned = sem("xs_turned")
        xd_made = sem("xd_made")
        scored = sem("scored")
        masked = sem("masked")
        cs_spread = sem("cs_spread")
        relu_done = sem("relu_done")
        decay_made = sem("decay_made")
        m_made = sem("m_made")
        y_done = sem("y_done")
        y_skip = sem("y_skip")
        y_gated = sem("y_gated")
        y_sq = sem("y_sq")
        gn_stat = sem("gn_stat")
        gn_rms = sem("gn_rms")
        gn_r = sem("gn_r")
        y_scaled = sem("y_scaled")
        y_hi = sem("y_hi")
        mix_lo = sem("mix_lo")
        ln_mean = sem("ln_mean")
        ln_cent = sem("ln_cent")
        ln_sq = sem("ln_sq")
        ln_var = sem("ln_var")
        ln_rms = sem("ln_rms")
        ln_r = sem("ln_r")
        ln_scaled = sem("ln_scaled")
        u_act = sem("u_act")
        u_hi = sem("u_hi")
        row_done = sem("row_done")
        mix_sq = sem("mix_sq")
        mix_g = sem("mix_g")
        row_sum = sem("row_sum")
        x_new = sem("x_new")
        silu_done = sem("silu_done")
        prod_done = sem("prod_done")
        hid_hi = sem("hid_hi")
        hid_lo = sem("hid_lo")
        down_done = sem("down_done")
        f_sq = sem("f_sq")
        f_g = sem("f_g")
        out_made = sem("out_made")
        stored = sem("stored")

        def pcol(name, i, n=1):
            return par[:, PAT[name] + i:PAT[name] + i + n]

        eps = stat[:, 0:1]
        ssq, rms, rstd = stat[:, 2:4], stat[:, 4:6], stat[:, 6:8]
        sq_part = stat[:, 8:16].rearrange("p (h c) -> p h c", c=NCH)

        def rows(w):
            return w.rearrange("(k p) n -> p k n", p=P)

        win_r, wout_r, gate_r, up_r, down_r = rows(w_in), rows(w_out), rows(w_gate), rows(w_up), rows(w_down)
        x_r = x.rearrange("(h p) d -> p h d", p=P)
        out_r = out.rearrange("(h p) d -> p h d", p=P)

        block = ctx.enter_context(nc.Block())

        @block.sync
        def _(sp):
            def load(q, i, k, src):
                if not (isinstance(q, int) and q == 0):
                    sp.wait_ge(lo_made, 4 * q + (i + 1 - SLOTS))
                sp.dma_start(raw[:, i, :].rearrange("p (k n) -> p k n", k=k), src).then_inc(unit_loaded[i], 16)

            def load_slab(q, w, col):
                for i in range(4):
                    load(q, i, 4, w[:, 4 * i:4 * i + 4, bass.ds(col, SLAB)])

            for h in range(TH):
                sp.dma_start(x_row[:, h, :], x_r[:, h, :]).then_inc(x_loaded[h], 16)
            sp.dma_start(dt_raw[:, :, :], win_r[:, :, COL_DT:COL_DT + HEADS]).then_inc(dtw_loaded, 16)
            load_slab(0, win_r, COL_A)
            load_slab(1, win_r, COL_GATE)
            with sp.Fori(1, PAIRS) as j:
                load_slab(2 * j, win_r, SLAB * j + COL_A)
                load_slab(2 * j + 1, win_r, SLAB * j + COL_GATE)
            with sp.Fori(0, XBC_SLABS) as m:
                load_slab(m + SLAB_X, win_r, SLAB * m + COL_XBC)
            with sp.Fori(0, Z_SLABS) as m:
                load_slab(m + SLAB_Z, win_r, SLAB * m + COL_Z)
            for n, (c, kp) in enumerate(WOUT_ORDER):
                load(QUAD_WOUT + n // 4, n % 4, 2, wout_r[:, 2 * kp:2 * kp + 2, 512 * c:512 * c + 512])
            with sp.Fori(0, FFN_PAIRS) as j:
                load_slab(2 * j + QUAD_FFN, gate_r, SLAB * j)
                load_slab(2 * j + (QUAD_FFN + 1), up_r, SLAB * j)
            sp.wait_ge(mix_g, TH * NCH)
            sp.dma_start(post_g[:, :], post_ffn.partition_broadcast(P)).then_inc(postg_loaded, 16)
            with sp.Fori(0, NCH // 2) as cp:
                for n in range(2 * DOWN_UNITS):
                    k, c = n % DOWN_UNITS, n // DOWN_UNITS
                    load(DOWN_UNITS // 2 * cp + (QUAD_DOWN + n // 4), n % 4, 2,
                         down_r[:, 2 * k:2 * k + 2, bass.ds(1024 * cp + 512 * c, 512)])
            for h in range(TH):
                sp.wait_ge(out_made, h + 1)
                sp.dma_start(out_r[:, h, :], f_row[:, h, :]).then_inc(stored, 16)
            sp.wait_ge(stored, 16 * TH)

        @block.gpsimd
        def _(pool):
            pool.memset(ident[:, :], 0.0).then_inc(consts, 1)
            pool.memset(sel[:, :, :], 0.0).then_inc(consts, 1)
            pool.memset(mask[:, :], 1.0).then_inc(consts, 1)
            pool.memset(mean_w[:, :], 1.0 / DC).then_inc(consts, 1)
            pool.memset(upad[:, :, 0:TAPS - 1], 0.0).then_inc(consts, 1)
            pool.memset(xpad[:, :, :, 0:TAPS4 - 1], 0.0).then_inc(consts, 1)
            pool.memset(stat[:, 0:1], EPS).then_inc(consts, 1)
            pool.memset(stat[:, 40:41], 0.0).then_inc(f_g, BANK_CREDIT)
            pool.wait_ge(consts, 7)
            pool.affine_select(out=ident[:, :], in_=ident[:, :], compare_op=ALU.not_equal, fill=1.0, base=0,
                               pattern=[[-1, P]], channel_multiplier=1).then_inc(consts, 1)
            pool.affine_select(out=sel[:, :, :], in_=sel[:, :, :], compare_op=ALU.not_equal, fill=1.0, base=0,
                               pattern=[[-1, HEADS], [0, P]], channel_multiplier=1).then_inc(consts, 1)
            pool.affine_select(out=mask[:, 0:T], in_=mask[:, 0:T], compare_op=ALU.is_ge, fill=0.0, base=0,
                               pattern=[[1, T]], channel_multiplier=-1).then_inc(consts, 1)
            pool.affine_select(out=mask[:, T:T + P], in_=mask[:, T:T + P], compare_op=ALU.is_ge, fill=0.0, base=0,
                               pattern=[[1, P]], channel_multiplier=-1).then_inc(consts, 1)
        CONSTS = 11

        @block.scalar
        def _(act):
            def hi(q, i):
                act.wait_ge(unit_loaded[i], 16 * q + 16)
                if not (isinstance(q, int) and q == 0):
                    act.wait_ge(multiplied, 4 * q + (i + 1 - SLOTS))
                act.activation(w_hi[:, i, :], raw[:, i, :], ACT.Copy).then_inc(hi_made, 1)

            def cross_copy(s, par_, off=4):
                act.wait_ge(multiplied, 4 * s + off)
                if not (isinstance(s, int) and s < 2):
                    act.wait_ge(summed, s - 1)
                b = 2 * par_
                act.activation(cross[:, par_, :, :], ps[:, b:b + 2, CROSS], ACT.Copy).then_inc(crossed, 1)

            def quad(q, before=None, after=None):
                hi(q, 0)
                hi(q, 1)
                hi(q, 2)
                if before:
                    before()
                hi(q, 3)
                if after:
                    after()

            def row_norm_start(n):
                for h in range(TH):
                    if n == 0:
                        act.wait_ge(x_loaded[h], 16)
                        if h == 0:
                            act.wait_ge(consts, CONSTS)
                    else:
                        act.wait_ge(x_new, h + 1)
                    act.activation(row_work[:, h, :], x_row[:, h, :], ACT.Square,
                                   accum_out=ssq[:, h:h + 1]).then_inc(row_sq, 1)
                for h in range(TH):
                    act.wait_ge(row_sq, TH * n + h + 1)
                    act.activation(rms[:, h:h + 1], ssq[:, h:h + 1], ACT.Sqrt, bias=eps, scale=1.0 / D).then_inc(row_rms, 1)

            def norm_split_hi(n, gain):
                for kp in range(KC // 2):
                    act.wait_ge(turned, n * (KC // 2) + kp + 1)
                    for k in range(2):
                        kc = 2 * kp + k
                        act.activation(acts[:, kc, 0, :], ps[:, 4 + kp % 4, k * T:k * T + T], ACT.Copy,
                                       scale=pcol(gain, kc)).then_inc(norm_hi, 1)

            act.dma_start(par[:, :], params).then_inc(par_loaded, 16)
            act.dma_start(post_g[:, :], post_mix.partition_broadcast(P)).then_inc(postg_loaded, 16)
            row_norm_start(0)
            act.wait_ge(dtw_loaded, 16)
            act.activation(dt_hi[:, :, :], dt_raw[:, :, :], ACT.Copy).then_inc(dtw_hi_made, 1)
            act.wait_ge(par_loaded, 16)
            norm_split_hi(0, "mix_g")
            hi(0, 0)
            hi(0, 1)
            hi(0, 2)
            hi(0, 3)
            act.wait_ge(dts, 2)
            act.activation(sm[:, 1, :], sm[:, 0, :], ACT.Abs).then_inc(dte, 1)
            act.wait_ge(dte, 1)
            act.activation(sm[:, 1, :], sm[:, 1, :], ACT.Exp, scale=-1.0).then_inc(dte, 1)
            act.activation(sm[:, 2, 0:HEADS], pcol("a_log", 0, HEADS), ACT.Exp).then_inc(dte, 1)

            def gate_sigmoid(j):
                act.wait_ge(summed, 2 * j + 2)
                act.activation(g_sum[:, :, :], g_sum[:, :, :], ACT.Sigmoid).then_inc(gate_sig, 1)

            def x_silu(m):
                act.wait_ge(xtap, 8 * m + 8)
                act.activation(xbc[:, bass.ds(2 * m, 2), :], xbc[:, bass.ds(2 * m, 2), :], ACT.Silu).then_inc(x_act, 1)

            def z_silu(m):
                act.wait_ge(summed, SLAB_Z + m + 1)
                act.activation(z[:, 2 * m:2 * m + 2, :], z[:, 2 * m:2 * m + 2, :], ACT.Silu).then_inc(z_act, 1)

            quad(1, lambda: cross_copy(0, 0))
            with act.Fori(1, PAIRS) as j:
                quad(2 * j, lambda: cross_copy(2 * j - 1, 1), lambda: gate_sigmoid(j - 1))
                quad(2 * j + 1, lambda: cross_copy(2 * j, 0))
            quad(SLAB_X, lambda: cross_copy(SLAB_X - 1, 1), lambda: gate_sigmoid(PAIRS - 1))
            quad(SLAB_X + 1, lambda: cross_copy(SLAB_X, 0), lambda: x_silu(0))
            with act.Fori(1, XBC_SLABS // 2) as m:
                quad(2 * m + SLAB_X, lambda: cross_copy(2 * m + (SLAB_X - 1), 1), lambda: x_silu(2 * m - 1))
                quad(2 * m + (SLAB_X + 1), lambda: cross_copy(2 * m + SLAB_X, 0), lambda: x_silu(2 * m))

            def decays(g):
                act.wait_ge(cs_spread, g + 1)
                if g >= 2:
                    act.wait_ge(y_done, g - 1)
                buf = decay[:, g % 2]
                for i in range(HPG):
                    h = HPG * g + i
                    row = ps[:, 4 + i // 2, (i % 2) * T:(i % 2) * T + T]
                    act.activation(buf[:, i, 0:T], row, ACT.Relu, bias=sm[:, 8, h:h + 1], scale=-1.0).then_inc(relu_done, 1)
                    act.activation(buf[:, i, T:T + P], row[:, P:T], ACT.Relu, bias=sm[:, 8, HEADS + h:HEADS + h + 1],
                                   scale=-1.0).then_inc(relu_done, 1)
                act.wait_ge(relu_done, 2 * HPG * (g + 1))
                act.activation(buf[:, :, :], buf[:, :, :], ACT.Exp, scale=-1.0).then_inc(decay_made, 1)

            quad(SLAB_Z, lambda: cross_copy(SLAB_Z - 1, 1), lambda: x_silu(XBC_SLABS - 1))
            decays(0)
            quad(SLAB_Z + 1, lambda: cross_copy(SLAB_Z, 0), lambda: z_silu(0))
            quad(SLAB_Z + 2, lambda: cross_copy(SLAB_Z + 1, 1), lambda: z_silu(1))
            quad(SLAB_Z + 3, lambda: cross_copy(SLAB_Z + 2, 0), lambda: z_silu(2))
            decays(1)
            quad(QUAD_WOUT, lambda: cross_copy(SLAB_Z + 3, 1), lambda: z_silu(3))
            decays(2)
            decays(3)
            act.wait_ge(ln_cent, 1)
            act.activation(upad[:, :, 0:T], u[:, :, :], ACT.Square).then_inc(ln_sq, 1)
            act.wait_ge(ln_var, 1)
            act.activation(g_sum[:, 0, :], ps[:, 5, 0:T], ACT.Sqrt, bias=eps).then_inc(ln_rms, 1)
            for g in range(GROUPS):
                act.wait_ge(y_gated, g + 1)
                act.activation(z[:, 2 * g:2 * g + 2, :], xbc[:, 2 * g:2 * g + 2, :], ACT.Square).then_inc(y_sq, 1)
            for g in range(GROUPS):
                act.wait_ge(gn_stat, g + 1)
                act.activation(scores[:, g, 0:T], ps[:, 4 + g, 0:T], ACT.Sqrt, bias=eps,
                               scale=float(GROUPS)).then_inc(gn_rms, 1)
            for m in range(SB):
                act.wait_ge(y_scaled, m // 2 + 1)
                if m == 0:
                    act.wait_ge(multiplied, 4 * QUAD_WOUT)
                act.activation(acts[:, CB + m, 0, :], xbc[:, m, :], ACT.Copy, scale=pcol("gn_w", m)).then_inc(y_hi, 1)
            act.wait_ge(ln_scaled, 1)
            for b in range(CB):
                act.activation(u[:, b, :], u[:, b, :], ACT.Silu, bias=pcol("ln_b", b), scale=pcol("ln_g", b)).then_inc(u_act, 1)
            act.wait_ge(u_act, CB)
            act.activation(acts[:, 0:CB, 0, :], u[:, :, :], ACT.Copy).then_inc(u_hi, 1)

            def mix_squares(c):
                act.wait_ge(multiplied, 4 * QUAD_WOUT + (LAST_OF_CHUNK[c] + 1))
                for h in range(TH):
                    act.activation(cross[:, h, :, :], ps[:, 2 * c + h, :], ACT.Square,
                                   accum_out=sq_part[:, h, c:c + 1]).then_inc(mix_sq, 1)
                    act.wait_ge(mix_sq, TH * c + h + 1)

            for n in range(4, len(WOUT_ORDER)):
                hi(QUAD_WOUT + n // 4, n % 4)
                if n == len(WOUT_ORDER) - 5:
                    for c in range(NCH - 1):
                        mix_squares(c)
            hi(QUAD_FFN, 0)
            hi(QUAD_FFN, 1)
            hi(QUAD_FFN, 2)
            mix_squares(NCH - 1)
            hi(QUAD_FFN, 3)
            act.wait_ge(row_sum, 1)
            act.activation(rms[:, :], ssq[:, :], ACT.Sqrt, bias=eps, scale=1.0 / D).then_inc(row_rms, 1)
            row_norm_start(1)
            norm_split_hi(1, "ffn_g")

            def ffn_silu(j):
                act.wait_ge(summed, 2 * j + (SLAB_FFN + 1))
                act.activation(g_sum[:, :, :], g_sum[:, :, :], ACT.Silu).then_inc(silu_done, 1)

            def hidden_hi(j):
                act.wait_ge(prod_done, j + 1)
                act.activation(hidden[:, bass.ds(2 * j, 2), 0, :], u_sum[:, :, :], ACT.Copy).then_inc(hid_hi, 1)

            quad(QUAD_FFN + 1, lambda: cross_copy(SLAB_FFN, 0, FFN_OFF), lambda: ffn_silu(0))
            with act.Fori(1, FFN_PAIRS) as j:
                quad(2 * j + QUAD_FFN, lambda: cross_copy(2 * j + (SLAB_FFN - 1), 1, FFN_OFF), lambda: hidden_hi(j - 1))
                quad(2 * j + (QUAD_FFN + 1), lambda: cross_copy(2 * j + SLAB_FFN, 0, FFN_OFF), lambda: ffn_silu(j))
            hi(QUAD_DOWN, 0)
            hi(QUAD_DOWN, 1)
            hi(QUAD_DOWN, 2)
            cross_copy(SLAB_FFN + 2 * FFN_PAIRS - 1, 1, FFN_OFF)
            hidden_hi(FFN_PAIRS - 1)

            def f_squares(c, cc):
                act.wait_ge(multiplied, 4 * QUAD_DOWN + DOWN_UNITS * (c + 1))
                for h in range(TH):
                    act.activation(cross[:, h, :, :], ps[:, 4 + 2 * cc + h, :], ACT.Square,
                                   accum_out=sq_part[:, h, c:c + 1]).then_inc(f_sq, 1)
                    act.wait_ge(f_sq, 2 * c + h + 1)

            def down_hi(cp, n0, n1):
                for n in range(n0, n1):
                    hi(DOWN_UNITS // 2 * cp + (QUAD_DOWN + n // 4), n % 4)

            down_hi(0, 3, DOWN_UNITS + 3)
            f_squares(0, 0)
            down_hi(0, DOWN_UNITS + 3, 2 * DOWN_UNITS)
            down_hi(1, 0, 3)
            f_squares(1, 1)
            down_hi(1, 3, DOWN_UNITS + 3)
            f_squares(2, 0)
            down_hi(1, DOWN_UNITS + 3, 2 * DOWN_UNITS)
            f_squares(3, 1)
            act.wait_ge(row_sum, 2)
            act.activation(rms[:, :], ssq[:, :], ACT.Sqrt, bias=eps, scale=1.0 / D).then_inc(row_rms, 1)

        @block.vector
        def _(dve):
            def lo(q, i):
                dve.wait_ge(hi_made, 4 * q + (i + 1))
                dve.tensor_tensor(w_lo[:, i, :], raw[:, i, :], w_hi[:, i, :].bitcast(F32), ALU.subtract).then_inc(lo_made, 1)

            def sum_slab(s, par_, dst, free_sem=None, free_at=None):
                if free_sem is not None:
                    dve.wait_ge(free_sem, free_at)
                dve.wait_ge(crossed, s + 1)
                b = 2 * par_
                dve.tensor_tensor(dst, ps[:, b:b + 2, MAIN], cross[:, par_, :, :], ALU.add).then_inc(summed, 1)

            def quad(q, f0=None, f1=None, before=None, after=None):
                lo(q, 0)
                if f0:
                    f0()
                lo(q, 1)
                if f1:
                    f1()
                lo(q, 2)
                if before:
                    before()
                lo(q, 3)
                if after:
                    after()

            def row_norm_finish(n):
                for h in range(TH):
                    dve.wait_ge(row_rms, (TH + 1) * n + h + 1)
                    dve.reciprocal(rstd[:, h:h + 1], rms[:, h:h + 1]).then_inc(row_rstd, 1)
                for h in range(TH):
                    dve.wait_ge(row_rstd, (TH + 1) * n + h + 1)
                    dve.tensor_scalar(row_work[:, h, :], x_row[:, h, :], rstd[:, h:h + 1], None, ALU.mult).then_inc(row_scaled, 1)

            def norm_split_lo(n, gain):
                for kp in range(KC // 2):
                    dve.wait_ge(norm_hi, n * KC + 2 * kp + 2)
                    for k in range(2):
                        kc = 2 * kp + k
                        dve.scalar_tensor_tensor(acts[:, kc, 1, :], ps[:, 4 + kp % 4, k * T:k * T + T], pcol(gain, kc),
                                                 acts[:, kc, 0, :].bitcast(F32), ALU.mult, ALU.subtract).then_inc(norm_lo, 1)

            row_norm_finish(0)
            dve.wait_ge(dtw_hi_made, 1)
            dve.tensor_tensor(dt_lo[:, :, :], dt_raw[:, :, :], dt_hi[:, :, :].bitcast(F32), ALU.subtract).then_inc(dtw_lo_made, 1)
            norm_split_lo(0, "mix_g")
            quad(0)

            dve.wait_ge(dt_done, TH)
            for h in range(TH):
                dve.tensor_tensor(sm[:, 0, h * HEADS:(h + 1) * HEADS], ps[:, 4 + h, 0:HEADS], pcol("dt_bias", 0, HEADS),
                                  ALU.add).then_inc(dts, 1)
            dve.wait_ge(dte, 3)
            step = [TH]

            def small(ins):
                ins.then_inc(dts, 1)
                step[0] += 1
                dve.wait_ge(dts, step[0])

            e_, s_, q_, acc = sm[:, 1, :], sm[:, 3, :], sm[:, 4, :], sm[:, 5, :]
            dt_t, a_t = sm[:, 6, :], sm[:, 7, :]
            small(dve.tensor_scalar(s_, e_, 2.0, None, ALU.add))
            small(dve.reciprocal(q_, s_))
            small(dve.tensor_tensor(s_, e_, q_, ALU.mult))
            small(dve.tensor_tensor(q_, s_, s_, ALU.mult))
            small(dve.tensor_scalar(acc, q_, SERIES[-1], None, ALU.mult))
            for c in SERIES[-2:0:-1]:
                small(dve.scalar_tensor_tensor(acc, acc, c, q_, ALU.add, ALU.mult))
            small(dve.scalar_tensor_tensor(acc, acc, 1.0, s_, ALU.add, ALU.mult))
            small(dve.tensor_scalar(s_, sm[:, 0, :], 0.0, None, ALU.max))
            small(dve.scalar_tensor_tensor(dt_t, acc, 2.0, s_, ALU.mult, ALU.add))
            for h in range(TH):
                dve.scalar_tensor_tensor(a_t[:, h * HEADS:(h + 1) * HEADS], dt_t[:, h * HEADS:(h + 1) * HEADS], -1.0,
                                         sm[:, 2, 0:HEADS], ALU.mult, ALU.mult).then_inc(a_ready, 1)

            def glu(j):
                dve.wait_ge(gate_sig, j + 1)
                dve.tensor_tensor(upad[:, bass.ds(2 * j, 2), TAPS - 1:PADW], u_sum[:, :, :], g_sum[:, :, :],
                                  ALU.mult).then_inc(glu_done, 1)

            def conv(n, b, k0, k1):
                for k in range(k0, k1):
                    src = upad[:, bass.ds(b, 1), k:k + T]
                    dst = u[:, bass.ds(b, 1), :]
                    w = par[:, bass.ds(b * TAPS + (PAT["dw_w"] + k), 1)]
                    if k == 0:
                        dve.tensor_scalar(dst, src, w, par[:, bass.ds(b + PAT["dw_b"], 1)], ALU.mult, ALU.add).then_inc(conv_tap, 1)
                    else:
                        dve.wait_ge(conv_tap, TAPS * n + k)
                        dve.scalar_tensor_tensor(dst, src, w, dst, ALU.mult, ALU.add).then_inc(conv_tap, 1)

            def x_after(m, par_):
                dve.wait_ge(summed, SLAB_X + m + 1)
                for k in range(TAPS4):
                    for b in range(2):
                        src = xpad[:, par_, b, k:k + T]
                        dst = xbc[:, bass.ds(2 * m + b, 1), :].rearrange("p a t -> p (a t)")
                        w = par[:, bass.ds((2 * m + b) * TAPS4 + (PAT["xw"] + k), 1)]
                        if k == 0:
                            dve.tensor_scalar(dst, src, w, par[:, bass.ds(2 * m + (b + PAT["xb"]), 1)],
                                              ALU.mult, ALU.add).then_inc(xtap, 1)
                        else:
                            dve.wait_ge(xtap, 8 * m + (2 * k - 1 + b))
                            dve.scalar_tensor_tensor(dst, src, w, dst, ALU.mult, ALU.add).then_inc(xtap, 1)

            def x_sum(m, par_):
                sum_slab(SLAB_X + m, par_, xpad[:, par_, :, TAPS4 - 1:XPW])

            quad(1, before=lambda: sum_slab(0, 0, u_sum[:, :, :]))
            dve.wait_ge(cs_done, 1)
            dve.tensor_copy(sm[:, 8, :], ps[:, 6, 0:2 * HEADS]).then_inc(cs_copied, 1)
            with dve.Fori(1, PAIRS) as j:
                quad(2 * j,
                     before=lambda: sum_slab(2 * j - 1, 1, g_sum[:, :, :]),
                     after=lambda: glu(j - 1))
                dve.wait_ge(glu_done, j)
                conv(j - 1, 2 * j - 2, 0, 8)
                quad(2 * j + 1,
                     f0=lambda: conv(j - 1, 2 * j - 2, 8, 16),
                     f1=lambda: conv(j - 1, 2 * j - 2, 16, 24),
                     before=lambda: sum_slab(2 * j, 0, u_sum[:, :, :], glu_done, j),
                     after=lambda: conv(j - 1, 2 * j - 2, 24, TAPS))
            dve.wait_ge(csT_done, 1)
            dve.tensor_copy(cs_row[:, :], ps[0:HEADS, 7, 0:T]).then_inc(csT_copied, 1)
            n0 = PAIRS - 1
            quad(SLAB_X, f0=lambda: conv(n0, 1, 0, 8), f1=lambda: conv(n0, 1, 8, 16),
                 before=lambda: sum_slab(SLAB_X - 1, 1, g_sum[:, :, :]), after=lambda: glu(PAIRS - 1))
            dve.wait_ge(glu_done, PAIRS)
            quad(SLAB_X + 1, f0=lambda: conv(n0, 1, 16, 24), f1=lambda: conv(n0, 1, 24, TAPS),
                 before=lambda: x_sum(0, 0), after=lambda: x_after(0, 0))
            with dve.Fori(1, XBC_SLABS // 2) as m:
                quad(2 * m + SLAB_X,
                     f0=lambda: conv(m + n0, 2 * m + 1, 0, 8), f1=lambda: conv(m + n0, 2 * m + 1, 8, 16),
                     before=lambda: x_sum(2 * m - 1, 1), after=lambda: x_after(2 * m - 1, 1))
                quad(2 * m + (SLAB_X + 1),
                     f0=lambda: conv(m + n0, 2 * m + 1, 16, 24), f1=lambda: conv(m + n0, 2 * m + 1, 24, TAPS),
                     before=lambda: x_sum(2 * m, 0), after=lambda: x_after(2 * m, 0))
            nl = CB - 1

            def z_sum(m):
                sum_slab(SLAB_Z + m, m % 2, z[:, 2 * m:2 * m + 2, :])

            def decayed_scores(g):
                dve.wait_ge(decay_made, g + 1)
                dve.tensor_tensor(decay[:, g % 2], decay[:, g % 2],
                                  scores[:, g:g + 1, :].to_broadcast([P, HPG, T + P]), ALU.mult).then_inc(m_made, 1)

            def skip(g):
                dve.wait_ge(y_done, g + 1)
                for b in range(2):
                    m = 2 * g + b
                    dve.scalar_tensor_tensor(xbc[:, m, :], xbc[:, m, :], pcol("d_skip", m), ps[:, 6 + b, 0:T],
                                             ALU.mult, ALU.add).then_inc(y_skip, 1)

            quad(SLAB_Z, f0=lambda: conv(nl, CB - 2, 0, 8), f1=lambda: conv(nl, CB - 2, 8, 16),
                 before=lambda: x_sum(XBC_SLABS - 1, 1), after=lambda: x_after(XBC_SLABS - 1, 1))
            quad(SLAB_Z + 1, f0=lambda: conv(nl, CB - 2, 16, 24), f1=lambda: conv(nl, CB - 2, 24, TAPS),
                 before=lambda: z_sum(0))
            for n in range(4):
                h, mq = n // 2, n % 2
                dve.wait_ge(xs_turned, n + 1)
                dve.tensor_tensor(xd[:, h, mq * 512:(mq + 1) * 512].rearrange("p (e d) -> p e d", d=HD),
                                  ps[:, 4 + n, :].rearrange("p (e d) -> p e d", d=HD),
                                  dt_t[:, h * HEADS + 8 * mq:h * HEADS + 8 * mq + 8].unsqueeze(2).to_broadcast([P, 8, HD]),
                                  ALU.mult).then_inc(xd_made, 1)
            quad(SLAB_Z + 2, before=lambda: z_sum(1))
            for g in range(GROUPS):
                dve.wait_ge(scored, g + 1)
                dve.tensor_tensor(scores[:, g, :], ps[:, 4 + g, 0:T + P], mask[:, :], ALU.mult).then_inc(masked, 1)
            dve.wait_ge(masked, GROUPS)
            decayed_scores(0)
            quad(SLAB_Z + 3, before=lambda: z_sum(2))
            skip(0)
            decayed_scores(1)
            quad(QUAD_WOUT, before=lambda: z_sum(3))
            skip(1)
            decayed_scores(2)
            dve.wait_ge(ln_mean, 1)
            dve.tensor_tensor(u[:, :, :], u[:, :, :], ps[:, 4:5, 0:T].to_broadcast([P, CB, T]), ALU.subtract).then_inc(ln_cent, 1)
            skip(2)
            decayed_scores(3)
            dve.wait_ge(ln_rms, 1)
            dve.reciprocal(g_sum[:, 1, :], g_sum[:, 0, :]).then_inc(ln_r, 1)
            skip(3)
            for g in range(GROUPS):
                if g == 0:
                    dve.wait_ge(z_act, Z_SLABS)
                dve.wait_ge(y_skip, 2 * g + 2)
                dve.tensor_tensor(xbc[:, 2 * g:2 * g + 2, :], xbc[:, 2 * g:2 * g + 2, :], z[:, 2 * g:2 * g + 2, :],
                                  ALU.mult).then_inc(y_gated, 1)
            dve.wait_ge(ln_r, 1)
            dve.tensor_tensor(u[:, :, :], u[:, :, :], g_sum[:, 1:2, :].to_broadcast([P, CB, T]), ALU.mult).then_inc(ln_scaled, 1)
            for g in range(GROUPS):
                dve.wait_ge(gn_rms, g + 1)
                dve.reciprocal(scores[:, g, 0:T], scores[:, g, 0:T]).then_inc(gn_r, 1)
                dve.wait_ge(gn_r, g + 1)
                dve.wait_ge(y_sq, g + 1)
                dve.tensor_tensor(xbc[:, 2 * g:2 * g + 2, :], xbc[:, 2 * g:2 * g + 2, :],
                                  scores[:, g:g + 1, 0:T].to_broadcast([P, 2, T]), ALU.mult).then_inc(y_scaled, 1)
            for m in range(SB):
                dve.wait_ge(y_hi, m + 1)
                dve.scalar_tensor_tensor(acts[:, CB + m, 1, :], xbc[:, m, :], pcol("gn_w", m),
                                         acts[:, CB + m, 0, :].bitcast(F32), ALU.mult, ALU.subtract).then_inc(mix_lo, 1)
            dve.wait_ge(u_hi, 1)
            dve.tensor_tensor(acts[:, 0:CB, 1, :], u[:, :, :], acts[:, 0:CB, 0, :].bitcast(F32), ALU.subtract).then_inc(mix_lo, 1)

            def scale_rows(c):
                dve.wait_ge(mix_sq, TH * c + TH)
                for h in range(TH):
                    dve.tensor_tensor(row_work[:, h, 512 * c:512 * c + 512], ps[:, 2 * c + h, :],
                                      post_g[:, 512 * c:512 * c + 512], ALU.mult).then_inc(mix_g, 1)

            for n in range(4, len(WOUT_ORDER)):
                lo(QUAD_WOUT + n // 4, n % 4)
                if n == len(WOUT_ORDER) - 5:
                    dve.wait_ge(postg_loaded, 16)
                    for c in range(NCH - 1):
                        scale_rows(c)
            lo(QUAD_FFN, 0)
            lo(QUAD_FFN, 1)
            lo(QUAD_FFN, 2)
            scale_rows(NCH - 1)
            dve.tensor_reduce(ssq[:, :], sq_part[:, :, :], mybir.AxisListType.X, ALU.add).then_inc(row_sum, 1)
            lo(QUAD_FFN, 3)
            dve.wait_ge(row_rms, TH + 1)
            dve.reciprocal(rstd[:, :], rms[:, :]).then_inc(row_rstd, 1)
            dve.wait_ge(row_rstd, TH + 1)
            dve.wait_ge(mix_g, TH * NCH)
            for h in range(TH):
                dve.scalar_tensor_tensor(x_row[:, h, :], row_work[:, h, :], rstd[:, h:h + 1], x_row[:, h, :],
                                         ALU.mult, ALU.add).then_inc(x_new, 1)
            row_norm_finish(1)
            norm_split_lo(1, "ffn_g")

            def product(j):
                dve.wait_ge(silu_done, j + 1)
                dve.wait_ge(summed, 2 * j + (SLAB_FFN + 2))
                dve.tensor_tensor(u_sum[:, :, :], u_sum[:, :, :], g_sum[:, :, :], ALU.mult).then_inc(prod_done, 1)

            def hidden_lo(j):
                dve.wait_ge(hid_hi, j + 1)
                dve.tensor_tensor(hidden[:, bass.ds(2 * j, 2), 1, :], u_sum[:, :, :],
                                  hidden[:, bass.ds(2 * j, 2), 0, :].bitcast(F32), ALU.subtract).then_inc(hid_lo, 1)

            def up_epilogue(j):
                if isinstance(j, int) and j == 0:
                    sum_slab(SLAB_FFN + 1, 1, u_sum[:, :, :])
                else:
                    sum_slab(2 * j + (SLAB_FFN + 1), 1, u_sum[:, :, :], hid_lo, j)
                product(j)

            quad(QUAD_FFN + 1, before=lambda: sum_slab(SLAB_FFN, 0, g_sum[:, :, :]))

            def ffn_pair(j, first):
                if first:
                    quad(2 * j + QUAD_FFN, before=lambda: up_epilogue(j - 1), after=lambda: hidden_lo(j - 1))
                    quad(2 * j + (QUAD_FFN + 1),
                         before=lambda: sum_slab(2 * j + SLAB_FFN, 0, g_sum[:, :, :], prod_done, j))
                else:
                    quad(2 * j + QUAD_FFN, before=lambda: up_epilogue(j - 1), after=lambda: hidden_lo(j - 1))
                    quad(2 * j + (QUAD_FFN + 1),
                         before=lambda: sum_slab(2 * j + SLAB_FFN, 0, g_sum[:, :, :], prod_done, j))

            ffn_pair(1, True)
            with dve.Fori(2, FFN_PAIRS) as j:
                ffn_pair(j, False)
            lo(QUAD_DOWN, 0)
            lo(QUAD_DOWN, 1)
            lo(QUAD_DOWN, 2)
            up_epilogue(FFN_PAIRS - 1)
            hidden_lo(FFN_PAIRS - 1)

            def scale_f(c):
                dve.wait_ge(f_sq, TH * c + TH)
                for h in range(TH):
                    dve.tensor_tensor(f_row[:, h, 512 * c:512 * c + 512], ps[:, 4 + 2 * (c % 2) + h, :],
                                      post_g[:, 512 * c:512 * c + 512], ALU.mult).then_inc(f_g, 1)

            def down_lo(cp, n0, n1):
                for n in range(n0, n1):
                    lo(DOWN_UNITS // 2 * cp + (QUAD_DOWN + n // 4), n % 4)

            down_lo(0, 3, DOWN_UNITS + 3)
            dve.wait_ge(postg_loaded, 32)
            scale_f(0)
            down_lo(0, DOWN_UNITS + 3, 2 * DOWN_UNITS)
            down_lo(1, 0, 3)
            scale_f(1)
            down_lo(1, 3, DOWN_UNITS + 3)
            scale_f(2)
            down_lo(1, DOWN_UNITS + 3, 2 * DOWN_UNITS)
            dve.wait_ge(f_sq, TH * NCH)
            dve.tensor_reduce(ssq[:, :], sq_part[:, :, :], mybir.AxisListType.X, ALU.add).then_inc(row_sum, 1)
            scale_f(3)
            dve.wait_ge(row_rms, 2 * TH + 2)
            dve.reciprocal(rstd[:, :], rms[:, :]).then_inc(row_rstd, 1)
            dve.wait_ge(row_rstd, 2 * TH + 2)
            dve.wait_ge(f_g, BANK_CREDIT + TH * NCH)
            for h in range(TH):
                dve.scalar_tensor_tensor(f_row[:, h, :], f_row[:, h, :], rstd[:, h:h + 1], x_row[:, h, :],
                                         ALU.mult, ALU.add).then_inc(out_made, 1)

        @block.tensor
        def _(pe):
            def slab(q, s, par_):
                if not (isinstance(s, int) and s < 2):
                    pe.wait_ge(summed, s - 1)
                b0 = 2 * par_
                for i in range(4):
                    pe.wait_ge(lo_made, 4 * q + (i + 1))
                    hi_t = w_hi[:, i, :].rearrange("p (k n) -> p k n", k=4)
                    lo_t = w_lo[:, i, :].rearrange("p (k n) -> p k n", k=4)
                    for b in range(2):
                        for k in range(4):
                            kc = 4 * i + k
                            pe.matmul(ps[:, b0 + b, :], hi_t[:, k, b * P:(b + 1) * P],
                                      acts[:, kc, :, :].rearrange("p a t -> p (a t)"), start=(kc == 0), stop=False)
                            last = pe.matmul(ps[:, b0 + b, MAIN], lo_t[:, k, b * P:(b + 1) * P], acts[:, kc, 0, :],
                                             start=False, stop=(kc == KC - 1))
                    last.then_inc(multiplied, 1)

            def turn_rows(n):
                for kp in range(KC // 2):
                    if kp >= 4:
                        pe.wait_ge(norm_lo, n * KC + 2 * (kp - 4) + 2)
                    for k in range(2):
                        kc = 2 * kp + k
                        for h in range(TH):
                            if kp == 0 and k == 0:
                                pe.wait_ge(row_scaled, TH * n + h + 1)
                            last = pe.transpose(ps[:, 4 + kp % 4, k * T + h * P:k * T + h * P + P],
                                                row_work[:, h, kc * P:(kc + 1) * P], ident[:, :])
                    last.then_inc(turned, 1)

            pe.wait_ge(consts, CONSTS)
            turn_rows(0)
            pe.wait_ge(norm_lo, KC)
            pe.wait_ge(dtw_lo_made, 1)
            for h in range(TH):
                for kc in range(KC):
                    xh = acts[:, kc, 0, h * P:(h + 1) * P]
                    xl = acts[:, kc, 1, h * P:(h + 1) * P]
                    pe.matmul(ps[:, 4 + h, 0:HEADS], xh, dt_hi[:, kc, :], start=(kc == 0), stop=False)
                    pe.matmul(ps[:, 4 + h, 0:HEADS], xh, dt_lo[:, kc, :], start=False, stop=False)
                    last = pe.matmul(ps[:, 4 + h, 0:HEADS], xl, dt_hi[:, kc, :], start=False, stop=(kc == KC - 1))
                last.then_inc(dt_done, 1)
            slab(0, 0, 0)
            pe.wait_ge(a_ready, TH)
            a_t = sm[:, 7, :]
            pe.matmul(ps[:, 6, 0:HEADS], mask[:, 0:P], a_t[:, 0:HEADS], start=True, stop=True)
            pe.matmul(ps[:, 6, HEADS:2 * HEADS], mask[:, P:T], a_t[:, 0:HEADS], start=True, stop=False)
            pe.matmul(ps[:, 6, HEADS:2 * HEADS], mask[:, 0:P], a_t[:, HEADS:2 * HEADS], start=False, stop=True).then_inc(cs_done, 1)
            slab(1, 1, 1)
            pe.wait_ge(cs_copied, 1)
            for h in range(TH):
                last = pe.transpose(ps[0:HEADS, 7, h * P:(h + 1) * P], sm[:, 8, h * HEADS:(h + 1) * HEADS], ident[:, :])
            last.then_inc(csT_done, 1)
            with pe.Fori(1, PAIRS) as j:
                slab(2 * j, 2 * j, 0)
                slab(2 * j + 1, 2 * j + 1, 1)
            with pe.Fori(0, XBC_SLABS // 2) as m:
                slab(2 * m + SLAB_X, 2 * m + SLAB_X, 0)
                slab(2 * m + (SLAB_X + 1), 2 * m + (SLAB_X + 1), 1)

            def spread_cs(g):
                for i in range(HPG):
                    last = pe.matmul(ps[:, 4 + i // 2, (i % 2) * T:(i % 2) * T + T], sel[:, HPG * g + i, :], cs_row[:, :],
                                     start=True, stop=True)
                last.then_inc(cs_spread, 1)

            def y_group(g):
                pe.wait_ge(m_made, g + 1)
                if g > 0:
                    pe.wait_ge(y_skip, 2 * g)
                for i in range(HPG):
                    h = HPG * g + i
                    o = ps[(i % 2) * HD:(i % 2) * HD + HD, 6 + i // 2, :]
                    pe.matmul(o[:, 0:T], xd[:, 0, h * HD:(h + 1) * HD], decay[:, g % 2, i, 0:T], start=True, stop=False)
                    last = pe.matmul(o[:, P:T], xd[:, 1, h * HD:(h + 1) * HD], decay[:, g % 2, i, T:T + P],
                                     start=False, stop=True)
                last.then_inc(y_done, 1)

            pe.wait_ge(csT_copied, 1)
            spread_cs(0)
            slab(SLAB_Z, SLAB_Z, 0)
            pe.wait_ge(x_act, XBC_SLABS)
            pe.wait_ge(decay_made, 1)
            for n in range(4):
                h, mq = n // 2, n % 2
                for i in range(4):
                    last = pe.transpose(ps[:, 4 + n, i * P:(i + 1) * P], xbc[:, 4 * mq + i, h * P:(h + 1) * P], ident[:, :])
                last.then_inc(xs_turned, 1)
            slab(SLAB_Z + 1, SLAB_Z + 1, 1)
            pe.wait_ge(xd_made, 4)
            for g in range(GROUPS):
                b, c = SB + g, SB + GROUPS + g
                pe.matmul(ps[:, 4 + g, 0:T], xbc[:, b, 0:P], xbc[:, c, :], start=True, stop=True)
                pe.matmul(ps[:, 4 + g, T:T + P], xbc[:, b, P:T], xbc[:, c, P:T], start=True, stop=True).then_inc(scored, 1)
            slab(SLAB_Z + 2, SLAB_Z + 2, 0)
            pe.wait_ge(masked, GROUPS)
            spread_cs(1)
            y_group(0)
            slab(SLAB_Z + 3, SLAB_Z + 3, 1)
            pe.wait_ge(relu_done, 2 * HPG * 2)
            spread_cs(2)
            y_group(1)
            pe.wait_ge(relu_done, 2 * HPG * 3)
            spread_cs(3)
            y_group(2)
            pe.wait_ge(relu_done, 2 * HPG * 4)
            pe.wait_ge(conv_tap, TAPS * CB)
            for b in range(CB):
                last = pe.matmul(ps[:, 4, 0:T], mean_w[:, :], u[:, b, :], start=(b == 0), stop=(b == CB - 1))
            last.then_inc(ln_mean, 1)
            y_group(3)
            pe.wait_ge(ln_sq, 1)
            for b in range(CB):
                last = pe.matmul(ps[:, 5, 0:T], mean_w[:, :], upad[:, b, 0:T], start=(b == 0), stop=(b == CB - 1))
            last.then_inc(ln_var, 1)
            for g in range(GROUPS):
                pe.wait_ge(y_sq, g + 1)
                if g == 0:
                    pe.wait_ge(ln_rms, 1)
                if g == 2:
                    pe.wait_ge(y_skip, SB)
                for b in range(2):
                    last = pe.matmul(ps[:, 4 + g, 0:T], mean_w[:, :], z[:, 2 * g + b, :], start=(b == 0), stop=(b == 1))
                last.then_inc(gn_stat, 1)

            pe.wait_ge(gn_rms, GROUPS)
            pe.wait_ge(summed, SLAB_FFN)
            for n, (c, kp) in enumerate(WOUT_ORDER):
                if n == 0:
                    pe.wait_ge(mix_lo, SB)
                if kp < CB // 2:
                    pe.wait_ge(mix_lo, SB + 1)
                pe.wait_ge(lo_made, 4 * QUAD_WOUT + n + 1)
                first = c == NCH - 1 and kp == 0 or c < NCH - 1 and kp == CB // 2
                last_k = c == NCH - 1 and kp == KC // 2 - 1 or c < NCH - 1 and kp == CB // 2 - 1
                for k in range(2):
                    for h in range(TH):
                        o = ps[:, 2 * c + h, :]
                        xh = acts[:, 2 * kp + k, 0, h * P:(h + 1) * P]
                        xl = acts[:, 2 * kp + k, 1, h * P:(h + 1) * P]
                        wh = w_hi[:, n % 4, k * 512:(k + 1) * 512]
                        wl = w_lo[:, n % 4, k * 512:(k + 1) * 512]
                        pe.matmul(o, xh, wh, start=(first and k == 0), stop=False)
                        pe.matmul(o, xh, wl, start=False, stop=False)
                        last = pe.matmul(o, xl, wh, start=False, stop=(last_k and k == 1))
                last.then_inc(multiplied, 1)

            pe.wait_ge(mix_g, TH * NCH)
            turn_rows(1)
            pe.wait_ge(norm_lo, 2 * KC)
            with pe.Fori(0, FFN_PAIRS) as j:
                slab(2 * j + QUAD_FFN, 2 * j + SLAB_FFN, 0)
                slab(2 * j + (QUAD_FFN + 1), 2 * j + (SLAB_FFN + 1), 1)

            with pe.Fori(0, NCH // 2) as cp:
                for n in range(2 * DOWN_UNITS):
                    kp, c = n % DOWN_UNITS, n // DOWN_UNITS
                    if kp == 0:
                        pe.wait_ge(f_g, 4 * cp + (2 * c + 1))
                        pe.wait_ge(hid_lo, FFN_PAIRS - 1)
                    if kp == DOWN_UNITS - 1:
                        pe.wait_ge(hid_lo, FFN_PAIRS)
                    pe.wait_ge(lo_made, 2 * DOWN_UNITS * cp + (4 * QUAD_DOWN + n + 1))
                    for k in range(2):
                        for h in range(TH):
                            o = ps[:, 4 + 2 * c + h, :]
                            xh = hidden[:, 2 * kp + k, 0, h * P:(h + 1) * P]
                            xl = hidden[:, 2 * kp + k, 1, h * P:(h + 1) * P]
                            wh = w_hi[:, n % 4, k * 512:(k + 1) * 512]
                            wl = w_lo[:, n % 4, k * 512:(k + 1) * 512]
                            pe.matmul(o, xh, wh, start=(kp == 0 and k == 0), stop=False)
                            pe.matmul(o, xh, wl, start=False, stop=False)
                            last = pe.matmul(o, xl, wh, start=False, stop=(kp == DOWN_UNITS - 1 and k == 1))
                    last.then_inc(multiplied, 1)


WOUT_ORDER = [(c, kp) for kp in list(range(CB // 2, KC // 2)) + list(range(CB // 2)) for c in range(NCH - 1)] + \
             [(NCH - 1, kp) for kp in range(KC // 2)]
LAST_OF_CHUNK = [max(n for n, (c, _) in enumerate(WOUT_ORDER) if c == chunk) for chunk in range(NCH)]


def kernel(**inputs):
    import numpy as np
    import concourse.bacc as bacc
    from concourse import mybir as _mybir
    from concourse.bass_utils import run_bass_kernel_spmd

    a = {n: np.ascontiguousarray(v) for n, v in inputs.items()}

    def chan(v):
        v = v.reshape(v.shape[0], -1)
        return v.reshape(v.shape[0] // P, P, -1).transpose(1, 0, 2).reshape(P, -1)

    cols = {
        "mix_g": chan(a["norm_mix_pre"][0]), "ffn_g": chan(a["norm_ffn_pre"][0]),
        "dw_w": chan(a["conv_dw_w"][0].T), "dw_b": chan(a["conv_dw_b"][0]),
        "ln_g": chan(a["conv_ln_g"][0]), "ln_b": chan(a["conv_ln_b"][0]),
        "xw": chan(a["ssd_conv_w"][0].T), "xb": chan(a["ssd_conv_b"][0]),
        "d_skip": chan(np.repeat(a["ssd_d"][0], HD)), "gn_w": chan(a["ssd_norm_w"][0]),
        "dt_bias": np.broadcast_to(a["ssd_dt_bias"][0], (P, HEADS)),
        "a_log": np.broadcast_to(a["ssd_a_log"][0], (P, HEADS)),
    }
    arrays = {
        "x": a["x"][0], "w_in": a["w_in"][0], "w_out": a["w_out"][0], "w_gate": a["w_gate"][0],
        "w_up": a["w_up"][0], "w_down": a["w_down"][0],
        "params": np.concatenate([cols[n] for n, _ in PCOLS], axis=1),
        "post_mix": a["norm_mix_post"][0], "post_ffn": a["norm_ffn_post"][0],
    }
    arrays = {"in_" + n: np.ascontiguousarray(v) for n, v in arrays.items()}
    nc = bacc.Bacc("TRN2", target_bir_lowering=False, num_devices=1)
    args = [nc.dram_tensor(n, v.shape, _mybir.dt.from_np(v.dtype), kind="ExternalInput").ap() for n, v in arrays.items()]
    out = nc.dram_tensor("out_x", (T, D), F32, kind="ExternalOutput").ap()
    build(nc, *args, out)
    r = run_bass_kernel_spmd(nc, [arrays], core_ids=[0])
    return r.results[0]["out_x"].reshape(1, T, D)
```

```python
from contextlib import ExitStack

import concourse.bass as bass
from concourse import mybir

F32 = mybir.dt.float32
F32R = mybir.dt.float32r
ACT = mybir.ActivationFunctionType
ALU = mybir.AluOpType

P = 128
T = 256
TH = T // P
D = 2048
KC = D // P
DC = 1024
DS = 1024
CB, SB = DC // P, DS // P
TAPS = 31
TAPS4 = 4
HEADS = 16
HD = 64
GROUPS = 4
HPG = HEADS // GROUPS
FF = 5632
FC = FF // P
EPS = 1e-6
SLOTS = 4
UNIT = 1024
SLAB = 256
MAIN, CROSS = slice(0, T), slice(T, 2 * T)

COL_A, COL_GATE, COL_Z, COL_XBC, COL_DT = 0, DC, 2 * DC, 2 * DC + DS, 2 * DC + DS + 2048
PAIRS = DC // SLAB
XBC_SLABS = 2048 // SLAB
Z_SLABS = DS // SLAB
SLAB_X = 2 * PAIRS
SLAB_Z = SLAB_X + XBC_SLABS
SLAB_FFN = SLAB_Z + Z_SLABS
FFN_PAIRS = FF // SLAB
QUAD_WOUT = SLAB_FFN
QUAD_FFN = QUAD_WOUT + D * D // (P * UNIT * 4)
QUAD_DOWN = QUAD_FFN + 2 * FFN_PAIRS
FFN_OFF = 4 * (QUAD_FFN - SLAB_FFN) + 4
DOWN_UNITS = FC // 2
NCH = D // 512
BANK_CREDIT = 3

SEG_A, SEG_B = 16, TAPS - 1 - 16
SEG_C = 14
AT_B = 2 * SEG_A * (PAIRS - 1)
AT_C = AT_B + 2 * SEG_B * (PAIRS - 1)
AT_D = AT_C + 2 * SEG_C
CONV_OPS = AT_D + 2 * (TAPS - 1 - SEG_C)
XOPS = 2 * (TAPS4 - 1)

PCOLS = [("mix_g", KC), ("ffn_g", KC), ("dw_w", CB * TAPS), ("dw_b", CB), ("ln_g", CB), ("ln_b", CB),
         ("xw", 16 * TAPS4), ("xb", 16), ("d_skip", SB), ("gn_w", SB), ("dt_bias", HEADS), ("a_log", HEADS)]
PAT, _n = {}, 0
for _name, _w in PCOLS:
    PAT[_name] = _n
    _n += _w
NPAR = _n

SERIES = [1.0 / (2 * i + 1) for i in range(9)]


def build(nc, x, w_in, w_out, w_gate, w_up, w_down, params, post_mix, post_ffn, out):
    ctx = ExitStack()
    with ctx:
        place = {"at": nc.sbuf_base}

        def sb(name, shape, dt=F32, at=None):
            size = 4
            for n in shape[1:]:
                size *= n
            size = -(-size // 32) * 32
            here = place["at"] if at is None else at
            if at is None:
                place["at"] += size
            return nc.alloc_sbuf_tensor_at(name, shape, dt, offset=here), here + size

        def keep(name, shape, dt=F32):
            return sb(name, shape, dt)[0]

        def sem(name):
            return ctx.enter_context(nc.semaphore(name))

        place["at"] = -(-place["at"] // 64) * 64
        raw = keep("raw", [P, SLOTS, UNIT])
        w_hi = keep("w_hi", [P, SLOTS, UNIT], F32R)
        w_lo = keep("w_lo", [P, SLOTS, UNIT], F32R)
        x_row = keep("x_row", [P, TH, D])
        acts_at = place["at"]
        acts = keep("acts", [P, KC, 2, T], F32R)
        post_g = keep("post_g", [P, D])
        par = keep("par", [P, NPAR])
        ident = keep("ident", [P, P])
        mean_w = keep("mean_w", [P, P])
        cross = keep("cross", [P, 2, 2, T])
        g_sum = keep("g_sum", [P, 2, T])
        u_sum = keep("u_sum", [P, 2, T])
        stat = keep("stat", [P, 48])
        phase = place["at"]
        hidden, end_ffn = sb("hidden", [P, FC, 2, T], F32R, phase)
        f_row, _ = sb("f_row", [P, TH, D], F32, acts_at)
        xbc, e = sb("xbc", [P, 16, T], F32, phase)
        row_work, _ = sb("row_work", [P, TH, D], F32, phase)
        PADW = T + TAPS - 1
        upad, e = sb("upad", [P, CB, PADW], F32, e)
        u, e = sb("u", [P, CB, T], F32, e)
        XPW = T + TAPS4 - 1
        xpad, e = sb("xpad", [P, 2, 2, XPW], F32, e)
        z_at = e
        z, e = sb("z", [P, SB, T], F32, e)
        sel, _ = sb("sel", [HEADS, HEADS, P], F32, z_at)
        xd, e = sb("xd", [P, TH, DS], F32, e)
        mask, e = sb("mask", [P, T + P], F32, e)
        scores, e = sb("scores", [P, GROUPS, T + P], F32, e)
        decay, e = sb("decay", [P, GROUPS, HPG, T + P], F32, e)
        cs_row, e = sb("cs_row", [HEADS, T], F32, e)
        dtw_at = e
        dt_raw, e = sb("dt_raw", [P, KC, HEADS], F32, e)
        dt_hi, e = sb("dt_hi", [P, KC, HEADS], F32R, e)
        dt_lo, e = sb("dt_lo", [P, KC, HEADS], F32R, e)
        sm, e = sb("sm", [P, 12, 2 * HEADS], F32, e)
        assert max(e, end_ffn) <= nc.sbuf_usable_end, (e, end_ffn, nc.sbuf_usable_end)

        ps = ctx.enter_context(nc.psum_tensor("ps", [P, 8, 512], F32))

        unit_loaded = [sem(f"unit_loaded{i}") for i in range(SLOTS)]
        x_loaded = [sem(f"x_loaded{i}") for i in range(TH)]
        par_loaded = sem("par_loaded")
        dtw_loaded = sem("dtw_loaded")
        postg_loaded = sem("postg_loaded")
        consts = sem("consts")
        hi_made = sem("hi_made")
        lo_made = sem("lo_made")
        multiplied = sem("multiplied")
        slab_done = sem("slab_done")
        crossed = sem("crossed")
        summed = sem("summed")
        row_sq = sem("row_sq")
        row_rms = sem("row_rms")
        row_rstd = sem("row_rstd")
        row_scaled = sem("row_scaled")
        turned = sem("turned")
        norm_hi = sem("norm_hi")
        norm_lo = sem("norm_lo")
        dt_done = sem("dt_done")
        dts = sem("dts")
        dte = sem("dte")
        dtw_hi_made = sem("dtw_hi_made")
        dtw_lo_made = sem("dtw_lo_made")
        a_ready = sem("a_ready")
        cs_done = sem("cs_done")
        cs_copied = sem("cs_copied")
        csT_done = sem("csT_done")
        csT_copied = sem("csT_copied")
        gate_sig = sem("gate_sig")
        glu_done = sem("glu_done")
        conv_first = sem("conv_first")
        x_first = sem("x_first")
        gn_spread = sem("gn_spread")
        ln_spread = sem("ln_spread")
        conv_tap = sem("conv_tap")
        xtap = sem("xtap")
        x_act = sem("x_act")
        z_act = sem("z_act")
        xs_turned = sem("xs_turned")
        xd_made = sem("xd_made")
        scored = sem("scored")
        masked = sem("masked")
        cs_spread = sem("cs_spread")
        relu_done = sem("relu_done")
        decay_made = sem("decay_made")
        m_made = sem("m_made")
        y_done = sem("y_done")
        y_skip = sem("y_skip")
        y_gated = sem("y_gated")
        y_sq = sem("y_sq")
        gn_stat = sem("gn_stat")
        gn_rms = sem("gn_rms")
        gn_r = sem("gn_r")
        y_scaled = sem("y_scaled")
        y_hi = sem("y_hi")
        mix_lo = sem("mix_lo")
        ln_mean = sem("ln_mean")
        ln_cent = sem("ln_cent")
        ln_sq = sem("ln_sq")
        ln_var = sem("ln_var")
        ln_rms = sem("ln_rms")
        ln_r = sem("ln_r")
        ln_scaled = sem("ln_scaled")
        u_act = sem("u_act")
        u_hi = sem("u_hi")
        row_done = sem("row_done")
        mix_sq = sem("mix_sq")
        mix_g = sem("mix_g")
        row_sum = sem("row_sum")
        x_new = sem("x_new")
        silu_done = sem("silu_done")
        prod_done = sem("prod_done")
        hid_hi = sem("hid_hi")
        hid_lo = sem("hid_lo")
        down_done = sem("down_done")
        f_sq = sem("f_sq")
        f_g = sem("f_g")
        out_made = sem("out_made")
        stored = sem("stored")

        def pcol(name, i, n=1):
            return par[:, PAT[name] + i:PAT[name] + i + n]

        eps = stat[:, 0:1]
        ssq, rms, rstd = stat[:, 2:4], stat[:, 4:6], stat[:, 6:8]
        gn_r8, ln_r2 = stat[:, 16:24], stat[:, 24:26]
        gn_m8, ln_m2 = stat[:, 26:34], stat[:, 34:36]
        sq_part = stat[:, 8:16].rearrange("p (h c) -> p h c", c=NCH)

        def rows(w):
            return w.rearrange("(k p) n -> p k n", p=P)

        win_r, wout_r, gate_r, up_r, down_r = rows(w_in), rows(w_out), rows(w_gate), rows(w_up), rows(w_down)
        x_r = x.rearrange("(h p) d -> p h d", p=P)
        out_r = out.rearrange("(h p) d -> p h d", p=P)

        block = ctx.enter_context(nc.Block())

        @block.sync
        def _(sp):
            def load(q, i, k, src):
                if not (isinstance(q, int) and q == 0):
                    sp.wait_ge(lo_made, 4 * q + (i + 1 - SLOTS))
                sp.dma_start(raw[:, i, :].rearrange("p (k n) -> p k n", k=k), src).then_inc(unit_loaded[i], 16)

            def load_slab(q, w, col):
                for i in range(4):
                    load(q, i, 4, w[:, 4 * i:4 * i + 4, bass.ds(col, SLAB)])

            for h in range(TH):
                sp.dma_start(x_row[:, h, :], x_r[:, h, :]).then_inc(x_loaded[h], 16)
            sp.dma_start(dt_raw[:, :, :], win_r[:, :, COL_DT:COL_DT + HEADS]).then_inc(dtw_loaded, 16)
            load_slab(0, win_r, COL_A)
            load_slab(1, win_r, COL_GATE)
            with sp.Fori(1, PAIRS) as j:
                load_slab(2 * j, win_r, SLAB * j + COL_A)
                load_slab(2 * j + 1, win_r, SLAB * j + COL_GATE)
            with sp.Fori(0, XBC_SLABS) as m:
                load_slab(m + SLAB_X, win_r, SLAB * m + COL_XBC)
            with sp.Fori(0, Z_SLABS) as m:
                load_slab(m + SLAB_Z, win_r, SLAB * m + COL_Z)
            for n, (c, kp) in enumerate(WOUT_ORDER):
                load(QUAD_WOUT + n // 4, n % 4, 2, wout_r[:, 2 * kp:2 * kp + 2, 512 * c:512 * c + 512])
            with sp.Fori(0, FFN_PAIRS) as j:
                load_slab(2 * j + QUAD_FFN, gate_r, SLAB * j)
                load_slab(2 * j + (QUAD_FFN + 1), up_r, SLAB * j)
            sp.wait_ge(mix_g, TH * NCH)
            sp.dma_start(post_g[:, :], post_ffn.partition_broadcast(P)).then_inc(postg_loaded, 16)
            with sp.Fori(0, NCH // 2) as cp:
                for n in range(2 * DOWN_UNITS):
                    k, c = n % DOWN_UNITS, n // DOWN_UNITS
                    load(DOWN_UNITS // 2 * cp + (QUAD_DOWN + n // 4), n % 4, 2,
                         down_r[:, 2 * k:2 * k + 2, bass.ds(1024 * cp + 512 * c, 512)])
            for h in range(TH):
                sp.wait_ge(out_made, h + 1)
                sp.dma_start(out_r[:, h, :], f_row[:, h, :]).then_inc(stored, 16)
            sp.wait_ge(stored, 16 * TH)

        @block.gpsimd
        def _(pool):
            pool.memset(ident[:, :], 0.0).then_inc(consts, 1)
            pool.memset(sel[:, :, :], 0.0).then_inc(consts, 1)
            pool.memset(mask[:, :], 1.0).then_inc(consts, 1)
            pool.memset(mean_w[:, :], 1.0 / DC).then_inc(consts, 1)
            pool.memset(upad[:, :, 0:TAPS - 1], 0.0).then_inc(consts, 1)
            pool.memset(xpad[:, :, :, 0:TAPS4 - 1], 0.0).then_inc(consts, 1)
            pool.memset(stat[:, 0:1], EPS).then_inc(consts, 1)
            pool.memset(stat[:, 40:41], 0.0).then_inc(f_g, BANK_CREDIT)
            pool.wait_ge(consts, 7)
            pool.affine_select(out=ident[:, :], in_=ident[:, :], compare_op=ALU.not_equal, fill=1.0, base=0,
                               pattern=[[-1, P]], channel_multiplier=1).then_inc(consts, 1)
            pool.affine_select(out=sel[:, :, :], in_=sel[:, :, :], compare_op=ALU.not_equal, fill=1.0, base=0,
                               pattern=[[-1, HEADS], [0, P]], channel_multiplier=1).then_inc(consts, 1)
            pool.affine_select(out=mask[:, 0:T], in_=mask[:, 0:T], compare_op=ALU.is_ge, fill=0.0, base=0,
                               pattern=[[1, T]], channel_multiplier=-1).then_inc(consts, 1)
            pool.affine_select(out=mask[:, T:T + P], in_=mask[:, T:T + P], compare_op=ALU.is_ge, fill=0.0, base=0,
                               pattern=[[1, P]], channel_multiplier=-1).then_inc(consts, 1)
        CONSTS = 11

        @block.scalar
        def _(act):
            def hi(q, i):
                act.wait_ge(unit_loaded[i], 16 * q + 16)
                if not (isinstance(q, int) and q == 0):
                    act.wait_ge(multiplied, 4 * q + (i + 1 - SLOTS))
                act.activation(w_hi[:, i, :], raw[:, i, :], ACT.Copy).then_inc(hi_made, 1)

            def cross_copy(s, par_, off=4):
                act.wait_ge(multiplied, 4 * s + off)
                if not (isinstance(s, int) and s < 2):
                    act.wait_ge(summed, s - 1)
                b = 2 * par_
                act.activation(cross[:, par_, :, :], ps[:, b:b + 2, CROSS], ACT.Copy).then_inc(crossed, 1)

            def quad(q, before=None, after=None, f0=None):
                hi(q, 0)
                if f0:
                    f0()
                hi(q, 1)
                hi(q, 2)
                if before:
                    before()
                hi(q, 3)
                if after:
                    after()

            def row_norm_start(n):
                for h in range(TH):
                    if n == 0:
                        act.wait_ge(x_loaded[h], 16)
                        if h == 0:
                            act.wait_ge(consts, CONSTS)
                    else:
                        act.wait_ge(x_new, h + 1)
                    act.activation(row_work[:, h, :], x_row[:, h, :], ACT.Square,
                                   accum_out=ssq[:, h:h + 1]).then_inc(row_sq, 1)
                for h in range(TH):
                    act.wait_ge(row_sq, TH * n + h + 1)
                    act.activation(rms[:, h:h + 1], ssq[:, h:h + 1], ACT.Sqrt, bias=eps, scale=1.0 / D).then_inc(row_rms, 1)

            def norm_split_hi(n, gain):
                for kp in range(KC // 2):
                    act.wait_ge(turned, n * (KC // 2) + kp + 1)
                    for k in range(2):
                        kc = 2 * kp + k
                        act.activation(acts[:, kc, 0, :], ps[:, 4 + kp % 4, k * T:k * T + T], ACT.Copy,
                                       scale=pcol(gain, kc)).then_inc(norm_hi, 1)

            act.dma_start(par[:, :], params).then_inc(par_loaded, 16)
            act.dma_start(post_g[:, :], post_mix.partition_broadcast(P)).then_inc(postg_loaded, 16)
            row_norm_start(0)
            for i in range(4):
                hi(0, i)
            act.wait_ge(par_loaded, 16)
            norm_split_hi(0, "mix_g")
            act.wait_ge(dtw_loaded, 16)
            act.activation(dt_hi[:, :, :], dt_raw[:, :, :], ACT.Copy).then_inc(dtw_hi_made, 1)

            def gate_sigmoid(j):
                act.wait_ge(summed, 2 * j + 2)
                act.activation(g_sum[:, :, :], g_sum[:, :, :], ACT.Sigmoid).then_inc(gate_sig, 1)

            def conv_start(j):
                act.wait_ge(glu_done, j + 1)
                for b in range(2):
                    act.activation(u[:, bass.ds(2 * j + b, 1), :], upad[:, bass.ds(2 * j + b, 1), 0:T], ACT.Identity,
                                   bias=par[:, bass.ds(2 * j + (b + PAT["dw_b"]), 1)],
                                   scale=par[:, bass.ds((2 * j + b) * TAPS + PAT["dw_w"], 1)]).then_inc(conv_first, 1)

            def x_start(m, par_):
                act.wait_ge(summed, SLAB_X + m + 1)
                for b in range(2):
                    act.activation(xbc[:, bass.ds(2 * m + b, 1), :], xpad[:, par_, b:b + 1, 0:T], ACT.Identity,
                                   bias=par[:, bass.ds(2 * m + (b + PAT["xb"]), 1)],
                                   scale=par[:, bass.ds((2 * m + b) * TAPS4 + PAT["xw"], 1)]).then_inc(x_first, 1)

            def x_silu(m):
                act.wait_ge(xtap, XOPS * m + XOPS)
                blocks = xbc_slabs[:, bass.ds(m, 1), :]
                act.activation(blocks, blocks, ACT.Silu).then_inc(x_act, 1)

            def z_silu(m):
                act.wait_ge(summed, SLAB_Z + m + 1)
                act.activation(z[:, 2 * m:2 * m + 2, :], z[:, 2 * m:2 * m + 2, :], ACT.Silu).then_inc(z_act, 1)

            def decays(g):
                act.wait_ge(cs_spread, g + 1)
                buf = decay[:, g]
                for i in range(HPG):
                    h = HPG * g + i
                    row = ps[:, 4 + 2 * (g % 2) + i // 2, (i % 2) * T:(i % 2) * T + T]
                    act.activation(buf[:, i, 0:T], row, ACT.Relu, bias=sm[:, 8, h:h + 1], scale=-1.0).then_inc(relu_done, 1)
                    act.activation(buf[:, i, T:T + P], row[:, P:T], ACT.Relu, bias=sm[:, 8, HEADS + h:HEADS + h + 1],
                                   scale=-1.0).then_inc(relu_done, 1)
                act.wait_ge(relu_done, 2 * HPG * (g + 1))
                act.activation(buf[:, :, :], buf[:, :, :], ACT.Exp, scale=-1.0).then_inc(decay_made, 1)

            xbc_slabs = xbc[:, :, :].rearrange("p (m b) t -> p m (b t)", b=2)
            quad(1, lambda: cross_copy(0, 0))
            act.wait_ge(dts, 2)
            act.activation(sm[:, 1, :], sm[:, 0, :], ACT.Abs).then_inc(dte, 1)
            act.wait_ge(dte, 1)
            act.activation(sm[:, 1, :], sm[:, 1, :], ACT.Exp, scale=-1.0).then_inc(dte, 1)
            act.activation(sm[:, 2, 0:HEADS], pcol("a_log", 0, HEADS), ACT.Exp).then_inc(dte, 1)
            with act.Fori(1, PAIRS) as j:
                quad(2 * j, lambda: cross_copy(2 * j - 1, 1), lambda: gate_sigmoid(j - 1))
                conv_start(j - 1)
                quad(2 * j + 1, lambda: cross_copy(2 * j, 0))
            quad(SLAB_X, lambda: cross_copy(SLAB_X - 1, 1), lambda: gate_sigmoid(PAIRS - 1))
            conv_start(PAIRS - 1)
            quad(SLAB_X + 1, lambda: cross_copy(SLAB_X, 0), lambda: x_start(0, 0))

            def x_pair(m, after0, after1):
                quad(2 * m + SLAB_X, lambda: cross_copy(2 * m + (SLAB_X - 1), 1), lambda: x_start(2 * m - 1, 1),
                     lambda: x_silu(2 * m - 2))
                if after0:
                    after0()
                quad(2 * m + (SLAB_X + 1), lambda: cross_copy(2 * m + SLAB_X, 0), lambda: x_start(2 * m, 0),
                     lambda: x_silu(2 * m - 1))
                if after1:
                    after1()

            with act.Fori(1, XBC_SLABS // 2 - 1) as m:
                x_pair(m, None, None)
            decays(0)
            x_pair(XBC_SLABS // 2 - 1, lambda: decays(1), lambda: decays(2))
            quad(SLAB_Z, lambda: cross_copy(SLAB_Z - 1, 1), lambda: x_start(XBC_SLABS - 1, 1), lambda: x_silu(XBC_SLABS - 2))
            decays(3)
            quad(SLAB_Z + 1, lambda: cross_copy(SLAB_Z, 0), lambda: z_silu(0), lambda: x_silu(XBC_SLABS - 1))
            quad(SLAB_Z + 2, lambda: cross_copy(SLAB_Z + 1, 1), lambda: z_silu(1))
            quad(SLAB_Z + 3, lambda: cross_copy(SLAB_Z + 2, 0), lambda: z_silu(2))

            def gated_squares(g):
                act.wait_ge(y_gated, g + 1)
                act.activation(z[:, 2 * g:2 * g + 2, :], xbc[:, 2 * g:2 * g + 2, :], ACT.Square).then_inc(y_sq, 1)

            gated_squares(0)
            gated_squares(1)
            quad(QUAD_WOUT, lambda: cross_copy(SLAB_Z + 3, 1), lambda: z_silu(3))
            gated_squares(2)
            gated_squares(3)
            act.wait_ge(gn_stat, 1)
            act.activation(gn_m8, ps[:, 4, T:T + 8], ACT.Sqrt, bias=eps, scale=float(GROUPS)).then_inc(gn_rms, 1)
            act.wait_ge(multiplied, 4 * QUAD_WOUT)
            for m in range(SB):
                act.wait_ge(y_scaled, m // 2 + 1)
                act.activation(acts[:, CB + m, 0, :], xbc[:, m, :], ACT.Copy, scale=pcol("gn_w", m)).then_inc(y_hi, 1)
            for n in range(4, 12):
                hi(QUAD_WOUT + n // 4, n % 4)
            act.wait_ge(ln_cent, 1)
            act.activation(upad[:, :, 0:T], u[:, :, :], ACT.Square).then_inc(ln_sq, 1)
            hi(QUAD_WOUT + 3, 0)
            act.wait_ge(ln_var, 1)
            act.activation(ln_m2, ps[:, 7, 0:TH], ACT.Sqrt, bias=eps).then_inc(ln_rms, 1)
            act.wait_ge(ln_scaled, 1)
            for b in range(CB):
                act.activation(u[:, b, :], u[:, b, :], ACT.Silu, bias=pcol("ln_b", b), scale=pcol("ln_g", b)).then_inc(u_act, 1)
                if b % 2:
                    act.wait_ge(u_act, b + 1)
                    act.activation(acts[:, b - 1:b + 1, 0, :], u[:, b - 1:b + 1, :], ACT.Copy).then_inc(u_hi, 1)

            def mix_squares(c):
                act.wait_ge(multiplied, 4 * QUAD_WOUT + (LAST_OF_CHUNK[c] + 1))
                for h in range(TH):
                    act.activation(cross[:, h, :, :], ps[:, 2 * c + h, :], ACT.Square,
                                   accum_out=sq_part[:, h, c:c + 1]).then_inc(mix_sq, 1)
                    act.wait_ge(mix_sq, TH * c + h + 1)

            for n in range(13, len(WOUT_ORDER)):
                hi(QUAD_WOUT + n // 4, n % 4)
                if n == len(WOUT_ORDER) - 5:
                    for c in range(NCH - 1):
                        mix_squares(c)
            hi(QUAD_FFN, 0)
            hi(QUAD_FFN, 1)
            hi(QUAD_FFN, 2)
            mix_squares(NCH - 1)
            hi(QUAD_FFN, 3)
            act.wait_ge(row_sum, 1)
            act.activation(rms[:, :], ssq[:, :], ACT.Sqrt, bias=eps, scale=1.0 / D).then_inc(row_rms, 1)
            row_norm_start(1)
            norm_split_hi(1, "ffn_g")

            def ffn_silu(j):
                act.wait_ge(summed, 2 * j + (SLAB_FFN + 1))
                act.activation(g_sum[:, :, :], g_sum[:, :, :], ACT.Silu).then_inc(silu_done, 1)

            def hidden_hi(j):
                act.wait_ge(prod_done, j + 1)
                act.activation(hidden[:, bass.ds(2 * j, 2), 0, :], u_sum[:, :, :], ACT.Copy).then_inc(hid_hi, 1)

            quad(QUAD_FFN + 1, lambda: cross_copy(SLAB_FFN, 0, FFN_OFF), lambda: ffn_silu(0))
            with act.Fori(1, FFN_PAIRS) as j:
                quad(2 * j + QUAD_FFN, lambda: cross_copy(2 * j + (SLAB_FFN - 1), 1, FFN_OFF), lambda: hidden_hi(j - 1))
                quad(2 * j + (QUAD_FFN + 1), lambda: cross_copy(2 * j + SLAB_FFN, 0, FFN_OFF), lambda: ffn_silu(j))
            hi(QUAD_DOWN, 0)
            hi(QUAD_DOWN, 1)
            hi(QUAD_DOWN, 2)
            cross_copy(SLAB_FFN + 2 * FFN_PAIRS - 1, 1, FFN_OFF)
            hidden_hi(FFN_PAIRS - 1)

            def f_squares(c, cc):
                act.wait_ge(multiplied, 4 * QUAD_DOWN + DOWN_UNITS * (c + 1))
                for h in range(TH):
                    act.activation(cross[:, h, :, :], ps[:, 4 + 2 * cc + h, :], ACT.Square,
                                   accum_out=sq_part[:, h, c:c + 1]).then_inc(f_sq, 1)
                    act.wait_ge(f_sq, 2 * c + h + 1)

            def down_hi(cp, n0, n1):
                for n in range(n0, n1):
                    hi(DOWN_UNITS // 2 * cp + (QUAD_DOWN + n // 4), n % 4)

            down_hi(0, 3, DOWN_UNITS + 3)
            f_squares(0, 0)
            down_hi(0, DOWN_UNITS + 3, 2 * DOWN_UNITS)
            down_hi(1, 0, 3)
            f_squares(1, 1)
            down_hi(1, 3, DOWN_UNITS + 3)
            f_squares(2, 0)
            down_hi(1, DOWN_UNITS + 3, 2 * DOWN_UNITS)
            f_squares(3, 1)
            act.wait_ge(row_sum, 2)
            act.activation(rms[:, :], ssq[:, :], ACT.Sqrt, bias=eps, scale=1.0 / D).then_inc(row_rms, 1)

        @block.vector
        def _(dve):
            def lo(q, i):
                dve.wait_ge(hi_made, 4 * q + (i + 1))
                dve.tensor_tensor(w_lo[:, i, :], raw[:, i, :], w_hi[:, i, :].bitcast(F32), ALU.subtract).then_inc(lo_made, 1)

            def sum_slab(s, par_, dst, free_sem=None, free_at=None):
                if free_sem is not None:
                    dve.wait_ge(free_sem, free_at)
                dve.wait_ge(crossed, s + 1)
                b = 2 * par_
                dve.tensor_tensor(dst, ps[:, b:b + 2, MAIN], cross[:, par_, :, :], ALU.add).then_inc(summed, 1)

            def quad(q, f0=None, f1=None, before=None, after=None):
                lo(q, 0)
                if f0:
                    f0()
                lo(q, 1)
                if f1:
                    f1()
                lo(q, 2)
                if before:
                    before()
                lo(q, 3)
                if after:
                    after()

            def row_norm_finish(n):
                for h in range(TH):
                    dve.wait_ge(row_rms, (TH + 1) * n + h + 1)
                    dve.reciprocal(rstd[:, h:h + 1], rms[:, h:h + 1]).then_inc(row_rstd, 1)
                for h in range(TH):
                    dve.wait_ge(row_rstd, (TH + 1) * n + h + 1)
                    dve.tensor_scalar(row_work[:, h, :], x_row[:, h, :], rstd[:, h:h + 1], None, ALU.mult).then_inc(row_scaled, 1)

            def norm_split_lo(n, gain):
                for kp in range(KC // 2):
                    dve.wait_ge(norm_hi, n * KC + 2 * kp + 2)
                    for k in range(2):
                        kc = 2 * kp + k
                        dve.scalar_tensor_tensor(acts[:, kc, 1, :], ps[:, 4 + kp % 4, k * T:k * T + T], pcol(gain, kc),
                                                 acts[:, kc, 0, :].bitcast(F32), ALU.mult, ALU.subtract).then_inc(norm_lo, 1)

            row_norm_finish(0)
            for i in range(4):
                lo(0, i)
            norm_split_lo(0, "mix_g")
            dve.wait_ge(dtw_hi_made, 1)
            dve.tensor_tensor(dt_lo[:, :, :], dt_raw[:, :, :], dt_hi[:, :, :].bitcast(F32), ALU.subtract).then_inc(dtw_lo_made, 1)
            quad(1, before=lambda: sum_slab(0, 0, u_sum[:, :, :]))

            dve.wait_ge(dt_done, TH)
            for h in range(TH):
                dve.tensor_tensor(sm[:, 0, h * HEADS:(h + 1) * HEADS], ps[:, 4 + h, 0:HEADS], pcol("dt_bias", 0, HEADS),
                                  ALU.add).then_inc(dts, 1)
            dve.wait_ge(dte, 3)
            step = [TH]

            def small(ins):
                ins.then_inc(dts, 1)
                step[0] += 1
                dve.wait_ge(dts, step[0])

            e_, s_, q_, acc = sm[:, 1, :], sm[:, 3, :], sm[:, 4, :], sm[:, 5, :]
            dt_t, a_t = sm[:, 6, :], sm[:, 7, :]
            small(dve.tensor_scalar(s_, e_, 2.0, None, ALU.add))
            small(dve.reciprocal(q_, s_))
            small(dve.tensor_tensor(s_, e_, q_, ALU.mult))
            small(dve.tensor_tensor(q_, s_, s_, ALU.mult))
            small(dve.tensor_scalar(acc, q_, SERIES[-1], None, ALU.mult))
            for c in SERIES[-2:0:-1]:
                small(dve.scalar_tensor_tensor(acc, acc, c, q_, ALU.add, ALU.mult))
            small(dve.scalar_tensor_tensor(acc, acc, 1.0, s_, ALU.add, ALU.mult))
            small(dve.tensor_scalar(s_, sm[:, 0, :], 0.0, None, ALU.max))
            small(dve.scalar_tensor_tensor(dt_t, acc, 2.0, s_, ALU.mult, ALU.add))
            for h in range(TH):
                dve.scalar_tensor_tensor(a_t[:, h * HEADS:(h + 1) * HEADS], dt_t[:, h * HEADS:(h + 1) * HEADS], -1.0,
                                         sm[:, 2, 0:HEADS], ALU.mult, ALU.mult).then_inc(a_ready, 1)

            def glu(j):
                dve.wait_ge(gate_sig, j + 1)
                dve.tensor_tensor(upad[:, bass.ds(2 * j, 2), TAPS - 1:PADW], u_sum[:, :, :], g_sum[:, :, :],
                                  ALU.mult).then_inc(glu_done, 1)

            def conv(pair, k0, k1, seg, at):
                for k in range(k0, k1):
                    for b in range(2):
                        if k > seg:
                            dve.wait_ge(conv_tap, at + (2 * (k - 1 - seg) + b + 1))
                        elif k == 1:
                            dve.wait_ge(conv_first, 2 * pair + (b + 1))
                        else:
                            dve.wait_ge(conv_tap, at)
                        dst = u[:, bass.ds(2 * pair + b, 1), :]
                        dve.scalar_tensor_tensor(dst, upad[:, bass.ds(2 * pair + b, 1), k:k + T],
                                                 par[:, bass.ds((2 * pair + b) * TAPS + (PAT["dw_w"] + k), 1)], dst,
                                                 ALU.mult, ALU.add).then_inc(conv_tap, 1)

            def x_after(m, par_):
                for k in range(1, TAPS4):
                    for b in range(2):
                        if k == 1:
                            dve.wait_ge(x_first, 2 * m + (b + 1))
                        else:
                            dve.wait_ge(xtap, XOPS * m + (2 * (k - 2) + b + 1))
                        dst = xbc[:, bass.ds(2 * m + b, 1), :]
                        dve.scalar_tensor_tensor(dst, xpad[:, par_, b:b + 1, k:k + T],
                                                 par[:, bass.ds((2 * m + b) * TAPS4 + (PAT["xw"] + k), 1)], dst,
                                                 ALU.mult, ALU.add).then_inc(xtap, 1)

            def x_sum(m, par_):
                sum_slab(SLAB_X + m, par_, xpad[:, par_, :, TAPS4 - 1:XPW])

            with dve.Fori(1, PAIRS) as j:
                quad(2 * j,
                     before=lambda: sum_slab(2 * j - 1, 1, g_sum[:, :, :]),
                     after=lambda: glu(j - 1))
                quad(2 * j + 1,
                     f0=lambda: conv(j - 1, 1, 6, 1, 2 * SEG_A * j - 2 * SEG_A),
                     f1=lambda: conv(j - 1, 6, 11, 1, 2 * SEG_A * j - 2 * SEG_A),
                     before=lambda: sum_slab(2 * j, 0, u_sum[:, :, :], glu_done, j),
                     after=lambda: conv(j - 1, 11, 1 + SEG_A, 1, 2 * SEG_A * j - 2 * SEG_A))
            K = 1 + SEG_A

            def seg_b(m, k0, k1):
                conv(m, k0, k1, K, 2 * SEG_B * m + AT_B)

            quad(SLAB_X, f0=lambda: seg_b(0, K, K + 4), f1=lambda: seg_b(0, K + 4, K + 8),
                 before=lambda: sum_slab(SLAB_X - 1, 1, g_sum[:, :, :]), after=lambda: glu(PAIRS - 1))
            dve.wait_ge(cs_done, 1)
            dve.tensor_copy(sm[:, 8, :], ps[:, 6, 0:2 * HEADS]).then_inc(cs_copied, 1)
            dve.wait_ge(glu_done, PAIRS)
            quad(SLAB_X + 1, f0=lambda: seg_b(0, K + 8, K + 11), f1=lambda: seg_b(0, K + 11, TAPS),
                 before=lambda: x_sum(0, 0), after=lambda: x_after(0, 0))
            dve.wait_ge(csT_done, 1)
            dve.tensor_copy(cs_row[:, :], ps[0:HEADS, 7, 0:T]).then_inc(csT_copied, 1)

            def x_pair(m, piece):
                quad(2 * m + SLAB_X, f0=lambda: piece(0), f1=lambda: piece(1),
                     before=lambda: x_sum(2 * m - 1, 1), after=lambda: x_after(2 * m - 1, 1))
                quad(2 * m + (SLAB_X + 1), f0=lambda: piece(2), f1=lambda: piece(3),
                     before=lambda: x_sum(2 * m, 0), after=lambda: x_after(2 * m, 0))

            B = [K, K + 4, K + 8, K + 11, TAPS]
            C = [1, 5, 9, 12, 1 + SEG_C]
            with dve.Fori(1, XBC_SLABS // 2 - 1) as m:
                x_pair(m, lambda i: seg_b(m, B[i], B[i + 1]))
            x_pair(XBC_SLABS // 2 - 1, lambda i: conv(PAIRS - 1, C[i], C[i + 1], 1, AT_C))

            def z_sum(m):
                sum_slab(SLAB_Z + m, m % 2, z[:, 2 * m:2 * m + 2, :])

            def decayed_scores(g):
                dve.wait_ge(decay_made, g + 1)
                dve.tensor_tensor(decay[:, g], decay[:, g],
                                  scores[:, g:g + 1, :].to_broadcast([P, HPG, T + P]), ALU.mult).then_inc(m_made, 1)

            def skip(g):
                dve.wait_ge(y_done, g + 1)
                for b in range(2):
                    m = 2 * g + b
                    dve.scalar_tensor_tensor(xbc[:, m, :], xbc[:, m, :], pcol("d_skip", m), ps[:, 4 + 2 * (g % 2) + b, 0:T],
                                             ALU.mult, ALU.add).then_inc(y_skip, 1)

            quad(SLAB_Z, before=lambda: x_sum(XBC_SLABS - 1, 1), after=lambda: x_after(XBC_SLABS - 1, 1))
            quad(SLAB_Z + 1, before=lambda: z_sum(0))
            for n in range(4):
                h, mq = n // 2, n % 2
                dve.wait_ge(xs_turned, n + 1)
                dve.tensor_tensor(xd[:, h, mq * 512:(mq + 1) * 512].rearrange("p (e d) -> p e d", d=HD),
                                  ps[:, 4 + n, :].rearrange("p (e d) -> p e d", d=HD),
                                  dt_t[:, h * HEADS + 8 * mq:h * HEADS + 8 * mq + 8].unsqueeze(2).to_broadcast([P, 8, HD]),
                                  ALU.mult).then_inc(xd_made, 1)
            quad(SLAB_Z + 2, before=lambda: z_sum(1))
            for g in range(GROUPS):
                dve.wait_ge(scored, g + 1)
                dve.tensor_tensor(scores[:, g, :], ps[:, 4 + g, 0:T + P], mask[:, :], ALU.mult).then_inc(masked, 1)
            dve.wait_ge(masked, GROUPS)
            decayed_scores(0)
            decayed_scores(1)
            quad(SLAB_Z + 3, f0=lambda: decayed_scores(2), f1=lambda: decayed_scores(3), before=lambda: z_sum(2))

            def gate(g):
                dve.wait_ge(z_act, g + 1)
                dve.wait_ge(y_skip, 2 * g + 2)
                dve.tensor_tensor(xbc[:, 2 * g:2 * g + 2, :], xbc[:, 2 * g:2 * g + 2, :], z[:, 2 * g:2 * g + 2, :],
                                  ALU.mult).then_inc(y_gated, 1)

            skip(0)
            skip(1)
            gate(0)
            gate(1)
            quad(QUAD_WOUT, before=lambda: z_sum(3))
            skip(2)
            skip(3)
            gate(2)
            gate(3)
            dve.wait_ge(gn_rms, 1)
            dve.reciprocal(gn_r8, gn_m8).then_inc(gn_r, 1)
            for g in range(GROUPS):
                dve.wait_ge(gn_spread, g // 2 + 1)
                dve.tensor_tensor(xbc[:, 2 * g:2 * g + 2, :], xbc[:, 2 * g:2 * g + 2, :],
                                  ps[:, 6 + g // 2:7 + g // 2, (g % 2) * T:(g % 2) * T + T].to_broadcast([P, 2, T]),
                                  ALU.mult).then_inc(y_scaled, 1)
            for m in range(SB):
                dve.wait_ge(y_hi, m + 1)
                dve.scalar_tensor_tensor(acts[:, CB + m, 1, :], xbc[:, m, :], pcol("gn_w", m),
                                         acts[:, CB + m, 0, :].bitcast(F32), ALU.mult, ALU.subtract).then_inc(mix_lo, 1)
            D_ = 1 + SEG_C
            for n in range(4, 12):
                lo(QUAD_WOUT + n // 4, n % 4)
                conv(PAIRS - 1, D_ + 2 * (n - 4), D_ + 2 * (n - 4) + 2, D_, AT_D)
            dve.wait_ge(ln_mean, 1)
            dve.tensor_tensor(u[:, :, :], u[:, :, :], ps[:, 6:7, 0:T].to_broadcast([P, CB, T]), ALU.subtract).then_inc(ln_cent, 1)
            lo(QUAD_WOUT + 3, 0)
            dve.wait_ge(ln_rms, 1)
            dve.reciprocal(ln_r2, ln_m2).then_inc(ln_r, 1)
            dve.wait_ge(ln_spread, 1)
            dve.wait_ge(ln_sq, 1)
            dve.tensor_tensor(u[:, :, :], u[:, :, :], ps[:, 7:8, T:2 * T].to_broadcast([P, CB, T]), ALU.mult).then_inc(ln_scaled, 1)
            for b in range(0, CB, 2):
                dve.wait_ge(u_hi, b // 2 + 1)
                dve.tensor_tensor(acts[:, b:b + 2, 1, :], u[:, b:b + 2, :], acts[:, b:b + 2, 0, :].bitcast(F32),
                                  ALU.subtract).then_inc(mix_lo, 1)

            def scale_rows(c):
                dve.wait_ge(mix_sq, TH * c + TH)
                for h in range(TH):
                    dve.tensor_tensor(row_work[:, h, 512 * c:512 * c + 512], ps[:, 2 * c + h, :],
                                      post_g[:, 512 * c:512 * c + 512], ALU.mult).then_inc(mix_g, 1)

            for n in range(13, len(WOUT_ORDER)):
                lo(QUAD_WOUT + n // 4, n % 4)
                if n == len(WOUT_ORDER) - 5:
                    dve.wait_ge(postg_loaded, 16)
                    for c in range(NCH - 1):
                        scale_rows(c)
            lo(QUAD_FFN, 0)
            lo(QUAD_FFN, 1)
            lo(QUAD_FFN, 2)
            scale_rows(NCH - 1)
            dve.tensor_reduce(ssq[:, :], sq_part[:, :, :], mybir.AxisListType.X, ALU.add).then_inc(row_sum, 1)
            lo(QUAD_FFN, 3)
            dve.wait_ge(row_rms, TH + 1)
            dve.reciprocal(rstd[:, :], rms[:, :]).then_inc(row_rstd, 1)
            dve.wait_ge(row_rstd, TH + 1)
            dve.wait_ge(mix_g, TH * NCH)
            for h in range(TH):
                dve.scalar_tensor_tensor(x_row[:, h, :], row_work[:, h, :], rstd[:, h:h + 1], x_row[:, h, :],
                                         ALU.mult, ALU.add).then_inc(x_new, 1)
            row_norm_finish(1)
            norm_split_lo(1, "ffn_g")

            def product(j):
                dve.wait_ge(silu_done, j + 1)
                dve.wait_ge(summed, 2 * j + (SLAB_FFN + 2))
                dve.tensor_tensor(u_sum[:, :, :], u_sum[:, :, :], g_sum[:, :, :], ALU.mult).then_inc(prod_done, 1)

            def hidden_lo(j):
                dve.wait_ge(hid_hi, j + 1)
                dve.tensor_tensor(hidden[:, bass.ds(2 * j, 2), 1, :], u_sum[:, :, :],
                                  hidden[:, bass.ds(2 * j, 2), 0, :].bitcast(F32), ALU.subtract).then_inc(hid_lo, 1)

            def up_epilogue(j):
                if isinstance(j, int) and j == 0:
                    sum_slab(SLAB_FFN + 1, 1, u_sum[:, :, :])
                else:
                    sum_slab(2 * j + (SLAB_FFN + 1), 1, u_sum[:, :, :], hid_lo, j)
                product(j)

            quad(QUAD_FFN + 1, before=lambda: sum_slab(SLAB_FFN, 0, g_sum[:, :, :]))

            def ffn_pair(j, first):
                if first:
                    quad(2 * j + QUAD_FFN, before=lambda: up_epilogue(j - 1), after=lambda: hidden_lo(j - 1))
                    quad(2 * j + (QUAD_FFN + 1),
                         before=lambda: sum_slab(2 * j + SLAB_FFN, 0, g_sum[:, :, :], prod_done, j))
                else:
                    quad(2 * j + QUAD_FFN, before=lambda: up_epilogue(j - 1), after=lambda: hidden_lo(j - 1))
                    quad(2 * j + (QUAD_FFN + 1),
                         before=lambda: sum_slab(2 * j + SLAB_FFN, 0, g_sum[:, :, :], prod_done, j))

            ffn_pair(1, True)
            with dve.Fori(2, FFN_PAIRS) as j:
                ffn_pair(j, False)
            lo(QUAD_DOWN, 0)
            lo(QUAD_DOWN, 1)
            lo(QUAD_DOWN, 2)
            up_epilogue(FFN_PAIRS - 1)
            hidden_lo(FFN_PAIRS - 1)

            def scale_f(c):
                dve.wait_ge(f_sq, TH * c + TH)
                for h in range(TH):
                    dve.tensor_tensor(f_row[:, h, 512 * c:512 * c + 512], ps[:, 4 + 2 * (c % 2) + h, :],
                                      post_g[:, 512 * c:512 * c + 512], ALU.mult).then_inc(f_g, 1)

            def down_lo(cp, n0, n1):
                for n in range(n0, n1):
                    lo(DOWN_UNITS // 2 * cp + (QUAD_DOWN + n // 4), n % 4)

            down_lo(0, 3, DOWN_UNITS + 3)
            dve.wait_ge(postg_loaded, 32)
            scale_f(0)
            down_lo(0, DOWN_UNITS + 3, 2 * DOWN_UNITS)
            down_lo(1, 0, 3)
            scale_f(1)
            down_lo(1, 3, DOWN_UNITS + 3)
            scale_f(2)
            down_lo(1, DOWN_UNITS + 3, 2 * DOWN_UNITS)
            dve.wait_ge(f_sq, TH * NCH)
            dve.tensor_reduce(ssq[:, :], sq_part[:, :, :], mybir.AxisListType.X, ALU.add).then_inc(row_sum, 1)
            scale_f(3)
            dve.wait_ge(row_rms, 2 * TH + 2)
            dve.reciprocal(rstd[:, :], rms[:, :]).then_inc(row_rstd, 1)
            dve.wait_ge(row_rstd, 2 * TH + 2)
            dve.wait_ge(f_g, BANK_CREDIT + TH * NCH)
            for h in range(TH):
                dve.scalar_tensor_tensor(f_row[:, h, :], f_row[:, h, :], rstd[:, h:h + 1], x_row[:, h, :],
                                         ALU.mult, ALU.add).then_inc(out_made, 1)

        @block.tensor
        def _(pe):
            def slab(q, s, par_, between=None):
                if not (isinstance(s, int) and s < 2):
                    pe.wait_ge(summed, s - 1)
                b0 = 2 * par_
                for i in range(4):
                    if between:
                        between(i)
                    pe.wait_ge(lo_made, 4 * q + (i + 1))
                    hi_t = w_hi[:, i, :].rearrange("p (k n) -> p k n", k=4)
                    lo_t = w_lo[:, i, :].rearrange("p (k n) -> p k n", k=4)
                    for b in range(2):
                        for k in range(4):
                            kc = 4 * i + k
                            pe.matmul(ps[:, b0 + b, :], hi_t[:, k, b * P:(b + 1) * P],
                                      acts[:, kc, :, :].rearrange("p a t -> p (a t)"), start=(kc == 0), stop=False)
                            last = pe.matmul(ps[:, b0 + b, MAIN], lo_t[:, k, b * P:(b + 1) * P], acts[:, kc, 0, :],
                                             start=False, stop=(kc == KC - 1))
                    last.then_inc(multiplied, 1)

            def turn_rows(n, k0, k1):
                for kp in range(k0, k1):
                    if kp >= 4:
                        pe.wait_ge(norm_lo, n * KC + 2 * (kp - 4) + 2)
                    for k in range(2):
                        kc = 2 * kp + k
                        for h in range(TH):
                            if kp == 0 and k == 0:
                                pe.wait_ge(row_scaled, TH * n + h + 1)
                            last = pe.transpose(ps[:, 4 + kp % 4, k * T + h * P:k * T + h * P + P],
                                                row_work[:, h, kc * P:(kc + 1) * P], ident[:, :])
                    last.then_inc(turned, 1)

            def first_slab(n, q, s):
                def ready(i):
                    if i in (1, 2):
                        turn_rows(n, 2 * i + 2, 2 * i + 4)
                    pe.wait_ge(norm_lo, n * KC + 4 * i + 4)
                turn_rows(n, 0, 4)
                slab(q, s, 0, ready)

            pe.wait_ge(consts, CONSTS)
            first_slab(0, 0, 0)
            pe.wait_ge(dtw_lo_made, 1)
            for h in range(TH):
                for kc in range(KC):
                    xh = acts[:, kc, 0, h * P:(h + 1) * P]
                    xl = acts[:, kc, 1, h * P:(h + 1) * P]
                    pe.matmul(ps[:, 4 + h, 0:HEADS], xh, dt_hi[:, kc, :], start=(kc == 0), stop=False)
                    pe.matmul(ps[:, 4 + h, 0:HEADS], xh, dt_lo[:, kc, :], start=False, stop=False)
                    last = pe.matmul(ps[:, 4 + h, 0:HEADS], xl, dt_hi[:, kc, :], start=False, stop=(kc == KC - 1))
                last.then_inc(dt_done, 1)
            slab(1, 1, 1)
            with pe.Fori(1, PAIRS) as j:
                slab(2 * j, 2 * j, 0)
                slab(2 * j + 1, 2 * j + 1, 1)
            pe.wait_ge(a_ready, TH)
            a_t = sm[:, 7, :]
            pe.matmul(ps[:, 6, 0:HEADS], mask[:, 0:P], a_t[:, 0:HEADS], start=True, stop=True)
            pe.matmul(ps[:, 6, HEADS:2 * HEADS], mask[:, P:T], a_t[:, 0:HEADS], start=True, stop=False)
            pe.matmul(ps[:, 6, HEADS:2 * HEADS], mask[:, 0:P], a_t[:, HEADS:2 * HEADS], start=False, stop=True).then_inc(cs_done, 1)
            slab(SLAB_X, SLAB_X, 0)
            pe.wait_ge(cs_copied, 1)
            for h in range(TH):
                last = pe.transpose(ps[0:HEADS, 7, h * P:(h + 1) * P], sm[:, 8, h * HEADS:(h + 1) * HEADS], ident[:, :])
            last.then_inc(csT_done, 1)
            slab(SLAB_X + 1, SLAB_X + 1, 1)
            with pe.Fori(1, XBC_SLABS // 2 - 1) as m:
                slab(2 * m + SLAB_X, 2 * m + SLAB_X, 0)
                slab(2 * m + (SLAB_X + 1), 2 * m + (SLAB_X + 1), 1)

            def spread_cs(g):
                for i in range(HPG):
                    last = pe.matmul(ps[:, 4 + 2 * (g % 2) + i // 2, (i % 2) * T:(i % 2) * T + T], sel[:, HPG * g + i, :], cs_row[:, :],
                                     start=True, stop=True)
                last.then_inc(cs_spread, 1)

            def y_group(g):
                pe.wait_ge(m_made, g + 1)
                if g >= 2:
                    pe.wait_ge(y_skip, 2 * (g - 1))
                for i in range(HPG):
                    h = HPG * g + i
                    o = ps[(i % 2) * HD:(i % 2) * HD + HD, 4 + 2 * (g % 2) + i // 2, :]
                    pe.matmul(o[:, 0:T], xd[:, 0, h * HD:(h + 1) * HD], decay[:, g, i, 0:T], start=True, stop=False)
                    last = pe.matmul(o[:, P:T], xd[:, 1, h * HD:(h + 1) * HD], decay[:, g, i, T:T + P],
                                     start=False, stop=True)
                last.then_inc(y_done, 1)

            pe.wait_ge(csT_copied, 1)
            spread_cs(0)
            spread_cs(1)
            slab(SLAB_X + XBC_SLABS - 2, SLAB_Z - 2, 0)
            pe.wait_ge(relu_done, 2 * HPG)
            spread_cs(2)
            slab(SLAB_X + XBC_SLABS - 1, SLAB_Z - 1, 1)
            pe.wait_ge(relu_done, 2 * 2 * HPG)
            spread_cs(3)
            slab(SLAB_Z, SLAB_Z, 0)
            pe.wait_ge(x_act, XBC_SLABS)
            pe.wait_ge(decay_made, GROUPS)
            for n in range(4):
                h, mq = n // 2, n % 2
                for i in range(4):
                    last = pe.transpose(ps[:, 4 + n, i * P:(i + 1) * P], xbc[:, 4 * mq + i, h * P:(h + 1) * P], ident[:, :])
                last.then_inc(xs_turned, 1)
            slab(SLAB_Z + 1, SLAB_Z + 1, 1)
            pe.wait_ge(xd_made, 4)
            for g in range(GROUPS):
                b, c = SB + g, SB + GROUPS + g
                pe.matmul(ps[:, 4 + g, 0:T], xbc[:, b, 0:P], xbc[:, c, :], start=True, stop=True)
                pe.matmul(ps[:, 4 + g, T:T + P], xbc[:, b, P:T], xbc[:, c, P:T], start=True, stop=True).then_inc(scored, 1)
            slab(SLAB_Z + 2, SLAB_Z + 2, 0)
            y_group(0)
            y_group(1)
            slab(SLAB_Z + 3, SLAB_Z + 3, 1)
            y_group(2)
            y_group(3)
            pe.wait_ge(y_skip, SB)
            for g in range(GROUPS):
                pe.wait_ge(y_sq, g + 1)
                for h in range(TH):
                    for b in range(2):
                        last = pe.matmul(ps[:, 4, T + TH * g + h:T + TH * g + h + 1], z[:, 2 * g + b, h * P:(h + 1) * P],
                                         mean_w[:, 0:1], start=(b == 0), stop=(b == 1))
            last.then_inc(gn_stat, 1)

            def spread(dst, col):
                return pe.matmul(dst, col.to_broadcast([P, P]), ident[:, :], start=True, stop=True)

            pe.wait_ge(gn_r, 1)
            for g in range(GROUPS):
                for h in range(TH):
                    o = (g % 2) * T + h * P
                    last = spread(ps[:, 6 + g // 2, o:o + P], gn_r8[:, TH * g + h:TH * g + h + 1])
                if g % 2:
                    last.then_inc(gn_spread, 1)

            def ln_mean_step():
                pe.wait_ge(conv_tap, CONV_OPS)
                pe.wait_ge(y_scaled, GROUPS)
                for b in range(CB):
                    last = pe.matmul(ps[:, 6, 0:T], mean_w[:, :], u[:, b, :], start=(b == 0), stop=(b == CB - 1))
                last.then_inc(ln_mean, 1)

            def ln_var_step():
                pe.wait_ge(ln_sq, 1)
                for h in range(TH):
                    for b in range(CB):
                        last = pe.matmul(ps[:, 7, h:h + 1], upad[:, b, h * P:(h + 1) * P], mean_w[:, 0:1],
                                         start=(b == 0), stop=(b == CB - 1))
                last.then_inc(ln_var, 1)
                pe.wait_ge(ln_r, 1)
                for h in range(TH):
                    last = spread(ps[:, 7, T + h * P:T + h * P + P], ln_r2[:, h:h + 1])
                last.then_inc(ln_spread, 1)

            pe.wait_ge(summed, SLAB_FFN)
            for n, (c, kp) in enumerate(WOUT_ORDER):
                if n == 11:
                    ln_mean_step()
                if n == 12:
                    ln_var_step()
                if c == 0 and kp >= CB // 2:
                    pe.wait_ge(mix_lo, 2 * (kp - CB // 2) + 2)
                if c == 0 and kp < CB // 2:
                    pe.wait_ge(mix_lo, SB + kp + 1)
                if n == 24:
                    pe.wait_ge(ln_scaled, 1)
                pe.wait_ge(lo_made, 4 * QUAD_WOUT + n + 1)
                first = c == NCH - 1 and kp == 0 or c < NCH - 1 and kp == CB // 2
                last_k = c == NCH - 1 and kp == KC // 2 - 1 or c < NCH - 1 and kp == CB // 2 - 1
                for k in range(2):
                    for h in range(TH):
                        o = ps[:, 2 * c + h, :]
                        xh = acts[:, 2 * kp + k, 0, h * P:(h + 1) * P]
                        xl = acts[:, 2 * kp + k, 1, h * P:(h + 1) * P]
                        wh = w_hi[:, n % 4, k * 512:(k + 1) * 512]
                        wl = w_lo[:, n % 4, k * 512:(k + 1) * 512]
                        pe.matmul(o, xh, wh, start=(first and k == 0), stop=False)
                        pe.matmul(o, xh, wl, start=False, stop=False)
                        last = pe.matmul(o, xl, wh, start=False, stop=(last_k and k == 1))
                last.then_inc(multiplied, 1)

            pe.wait_ge(mix_g, TH * NCH)
            first_slab(1, QUAD_FFN, SLAB_FFN)
            slab(QUAD_FFN + 1, SLAB_FFN + 1, 1)
            with pe.Fori(1, FFN_PAIRS) as j:
                slab(2 * j + QUAD_FFN, 2 * j + SLAB_FFN, 0)
                slab(2 * j + (QUAD_FFN + 1), 2 * j + (SLAB_FFN + 1), 1)

            with pe.Fori(0, NCH // 2) as cp:
                for n in range(2 * DOWN_UNITS):
                    kp, c = n % DOWN_UNITS, n // DOWN_UNITS
                    if kp == 0:
                        pe.wait_ge(f_g, 4 * cp + (2 * c + 1))
                        pe.wait_ge(hid_lo, FFN_PAIRS - 1)
                    if kp == DOWN_UNITS - 1:
                        pe.wait_ge(hid_lo, FFN_PAIRS)
                    pe.wait_ge(lo_made, 2 * DOWN_UNITS * cp + (4 * QUAD_DOWN + n + 1))
                    for k in range(2):
                        for h in range(TH):
                            o = ps[:, 4 + 2 * c + h, :]
                            xh = hidden[:, 2 * kp + k, 0, h * P:(h + 1) * P]
                            xl = hidden[:, 2 * kp + k, 1, h * P:(h + 1) * P]
                            wh = w_hi[:, n % 4, k * 512:(k + 1) * 512]
                            wl = w_lo[:, n % 4, k * 512:(k + 1) * 512]
                            pe.matmul(o, xh, wh, start=(kp == 0 and k == 0), stop=False)
                            pe.matmul(o, xh, wl, start=False, stop=False)
                            last = pe.matmul(o, xl, wh, start=False, stop=(kp == DOWN_UNITS - 1 and k == 1))
                    last.then_inc(multiplied, 1)


WOUT_ORDER = [(c, kp) for kp in list(range(CB // 2, KC // 2)) + list(range(CB // 2)) for c in range(NCH - 1)] + \
             [(NCH - 1, kp) for kp in range(KC // 2)]
LAST_OF_CHUNK = [max(n for n, (c, _) in enumerate(WOUT_ORDER) if c == chunk) for chunk in range(NCH)]


def kernel(**inputs):
    import numpy as np
    import concourse.bacc as bacc
    from concourse import mybir as _mybir
    from concourse.bass_utils import run_bass_kernel_spmd

    a = {n: np.ascontiguousarray(v) for n, v in inputs.items()}

    def chan(v):
        v = v.reshape(v.shape[0], -1)
        return v.reshape(v.shape[0] // P, P, -1).transpose(1, 0, 2).reshape(P, -1)

    cols = {
        "mix_g": chan(a["norm_mix_pre"][0]), "ffn_g": chan(a["norm_ffn_pre"][0]),
        "dw_w": chan(a["conv_dw_w"][0].T), "dw_b": chan(a["conv_dw_b"][0]),
        "ln_g": chan(a["conv_ln_g"][0]), "ln_b": chan(a["conv_ln_b"][0]),
        "xw": chan(a["ssd_conv_w"][0].T), "xb": chan(a["ssd_conv_b"][0]),
        "d_skip": chan(np.repeat(a["ssd_d"][0], HD)), "gn_w": chan(a["ssd_norm_w"][0]),
        "dt_bias": np.broadcast_to(a["ssd_dt_bias"][0], (P, HEADS)),
        "a_log": np.broadcast_to(a["ssd_a_log"][0], (P, HEADS)),
    }
    arrays = {
        "x": a["x"][0], "w_in": a["w_in"][0], "w_out": a["w_out"][0], "w_gate": a["w_gate"][0],
        "w_up": a["w_up"][0], "w_down": a["w_down"][0],
        "params": np.concatenate([cols[n] for n, _ in PCOLS], axis=1),
        "post_mix": a["norm_mix_post"][0], "post_ffn": a["norm_ffn_post"][0],
    }
    arrays = {"in_" + n: np.ascontiguousarray(v) for n, v in arrays.items()}
    nc = bacc.Bacc("TRN2", target_bir_lowering=False, num_devices=1)
    args = [nc.dram_tensor(n, v.shape, _mybir.dt.from_np(v.dtype), kind="ExternalInput").ap() for n, v in arrays.items()]
    out = nc.dram_tensor("out_x", (T, D), F32, kind="ExternalOutput").ap()
    build(nc, *args, out)
    r = run_bass_kernel_spmd(nc, [arrays], core_ids=[0])
    return r.results[0]["out_x"].reshape(1, T, D)
```

```python
from contextlib import ExitStack

import concourse.bass as bass
from concourse import mybir

F32 = mybir.dt.float32
F32R = mybir.dt.float32r
ACT = mybir.ActivationFunctionType
ALU = mybir.AluOpType

P = 128
T = 256
TH = T // P
D = 2048
KC = D // P
DC = 1024
DS = 1024
CB, SB = DC // P, DS // P
TAPS = 31
TAPS4 = 4
HEADS = 16
HD = 64
GROUPS = 4
HPG = HEADS // GROUPS
FF = 5632
FC = FF // P
EPS = 1e-6
SLOTS = 4
UNIT = 1024
SLAB = 256
MAIN, CROSS = slice(0, T), slice(T, 2 * T)

COL_A, COL_GATE, COL_Z, COL_XBC, COL_DT = 0, DC, 2 * DC, 2 * DC + DS, 2 * DC + DS + 2048
PAIRS = DC // SLAB
XBC_SLABS = 2048 // SLAB
Z_SLABS = DS // SLAB
SLAB_X = 2 * PAIRS
SLAB_Z = SLAB_X + XBC_SLABS
FFN_PAIRS = FF // SLAB
QUAD_WOUT = SLAB_Z + Z_SLABS
QUAD_FFN = QUAD_WOUT + D * D // (P * UNIT * 4)
QUAD_DOWN = QUAD_FFN + 2 * FFN_PAIRS
DOWN_UNITS = FC // 2
NCH = D // 512
OUT_PARTS = [slice(0, 1024), slice(1024, 1536), slice(1536, D)]
BANK_CREDIT = 3
U_UNIT = (NCH - 1) * SB // 2
AT_MEAN, AT_VAR, AT_SPREAD = 5, 8, 9

SEG_A, SEG_B = 16, TAPS - 1 - 16
SEG_C = 10
AT_B = 2 * SEG_A * (PAIRS - 1)
AT_C = AT_B + 2 * SEG_B * (PAIRS - 1)
AT_D = AT_C + 2 * SEG_C
CONV_OPS = AT_D + 2 * (TAPS - 1 - SEG_C)
XOPS = 2 * (TAPS4 - 1)

PCOLS = [("mix_g", KC), ("ffn_g", KC), ("dw_w", CB * TAPS), ("dw_b", CB), ("ln_g", CB), ("ln_b", CB),
         ("xw", 16 * TAPS4), ("xb", 16), ("d_skip", SB), ("gn_w", SB), ("dt_bias", HEADS), ("a_log", HEADS)]
PAT, _n = {}, 0
for _name, _w in PCOLS:
    PAT[_name] = _n
    _n += _w
NPAR = _n

SERIES = [1.0 / (2 * i + 1) for i in range(9)]


def build(nc, x, w_in, w_out, w_gate, w_up, w_down, params, post_mix, post_ffn, out):
    ctx = ExitStack()
    with ctx:
        place = {"at": nc.sbuf_base}

        def sb(name, shape, dt=F32, at=None):
            size = 4
            for n in shape[1:]:
                size *= n
            size = -(-size // 32) * 32
            here = place["at"] if at is None else at
            if at is None:
                place["at"] += size
            return nc.alloc_sbuf_tensor_at(name, shape, dt, offset=here), here + size

        def keep(name, shape, dt=F32):
            return sb(name, shape, dt)[0]

        def sem(name):
            return ctx.enter_context(nc.semaphore(name))

        place["at"] = -(-place["at"] // 64) * 64
        raw = keep("raw", [P, SLOTS, UNIT])
        w_hi = keep("w_hi", [P, SLOTS, UNIT], F32R)
        w_lo = keep("w_lo", [P, SLOTS, UNIT], F32R)
        x_row = keep("x_row", [P, TH, D])
        acts_at = place["at"]
        acts = keep("acts", [P, KC, 2, T], F32R)
        post_g = keep("post_g", [P, D])
        par = keep("par", [P, NPAR])
        ident = keep("ident", [P, P])
        mean_w = keep("mean_w", [P, P])
        cross = keep("cross", [P, 2, 2, T])
        gate_buf = keep("gate_buf", [P, 2, T])
        up_buf = keep("up_buf", [P, 2, T])
        stat = keep("stat", [P, 48])
        diag = keep("diag", [P, TH, P])
        phase = place["at"]
        hidden, end_ffn = sb("hidden", [P, FC, 2, T], F32R, phase)
        f_row, _ = sb("f_row", [P, TH, D], F32, acts_at)
        xbc, e = sb("xbc", [P, 16, T], F32, phase)
        row_work, _ = sb("row_work", [P, TH, D], F32, phase)
        PADW = T + TAPS - 1
        upad, e = sb("upad", [P, CB, PADW], F32, e)
        u, e = sb("u", [P, CB, T], F32, e)
        XPW = T + TAPS4 - 1
        xpad, e = sb("xpad", [P, 2, 2, XPW], F32, e)
        z_at = e
        z, e = sb("z", [P, SB, T], F32, e)
        sel, _ = sb("sel", [HEADS, HEADS, P], F32, z_at)
        xd, e = sb("xd", [P, TH, DS], F32, e)
        mask, e = sb("mask", [P, T + P], F32, e)
        scores, e = sb("scores", [P, GROUPS, T + P], F32, e)
        decay, e = sb("decay", [P, GROUPS, HPG, T + P], F32, e)
        cs_row, e = sb("cs_row", [HEADS, T], F32, e)
        dt_raw, e = sb("dt_raw", [P, KC, HEADS], F32, e)
        dt_w, e = sb("dt_w", [P, KC, 2, HEADS], F32R, e)
        dt_row, e = sb("dt_row", [2 * HEADS, 2 * T], F32, e)
        sm, e = sb("sm", [P, 9, 2 * HEADS], F32, e)
        dt_v, dt_e, a_exp, ser_s, ser_q, ser_acc, dt_tab, a_tab, cs_tab = (sm[:, i, :] for i in range(9))
        assert max(e, end_ffn) <= nc.sbuf_usable_end, (e, end_ffn, nc.sbuf_usable_end)

        ps = ctx.enter_context(nc.psum_tensor("ps", [P, 8, 512], F32))

        unit_loaded = [sem(f"unit_loaded{i}") for i in range(SLOTS)]
        x_loaded = [sem(f"x_loaded{i}") for i in range(TH)]
        par_loaded = sem("par_loaded")
        dtw_loaded = sem("dtw_loaded")
        postg_loaded = sem("postg_loaded")
        stored = sem("stored")
        hi_made = sem("hi_made")
        lo_made = sem("lo_made")
        multiplied = sem("multiplied")
        eps_set = sem("eps_set")
        consts = sem("consts")
        warmed = sem("warmed")
        row_sq = sem("row_sq")
        row_sum = sem("row_sum")
        row_rms = sem("row_rms")
        row_rstd = sem("row_rstd")
        diag_made = sem("diag_made")
        turned = sem("turned")
        norm_hi = sem("norm_hi")
        norm_lo = sem("norm_lo")
        dtw_hi_made = sem("dtw_hi_made")
        dtw_lo_made = sem("dtw_lo_made")
        dt_done = sem("dt_done")
        dt_copied = sem("dt_copied")
        dt_turned = sem("dt_turned")
        dt_step = sem("dt_step")
        dt_exp = sem("dt_exp")
        a_ready = sem("a_ready")
        cs_done = sem("cs_done")
        cs_copied = sem("cs_copied")
        csT_done = sem("csT_done")
        csT_copied = sem("csT_copied")
        cs_spread = sem("cs_spread")
        relu_done = sem("relu_done")
        decay_made = sem("decay_made")
        gate_sig = sem("gate_sig")
        glu_done = sem("glu_done")
        conv_first = sem("conv_first")
        conv_tap = sem("conv_tap")
        x_first = sem("x_first")
        x_in = sem("x_in")
        x_tap = sem("x_tap")
        x_act = sem("x_act")
        z_act = sem("z_act")
        xs_turned = sem("xs_turned")
        xd_made = sem("xd_made")
        scored = sem("scored")
        masked = sem("masked")
        scores_decayed = sem("scores_decayed")
        y_done = sem("y_done")
        y_skip = sem("y_skip")
        y_gated = sem("y_gated")
        y_sq = sem("y_sq")
        gn_stat = sem("gn_stat")
        gn_rms = sem("gn_rms")
        gn_inverse = sem("gn_inverse")
        gn_spread = sem("gn_spread")
        y_scaled = sem("y_scaled")
        y_hi = sem("y_hi")
        ln_mean = sem("ln_mean")
        ln_cent = sem("ln_cent")
        ln_sq = sem("ln_sq")
        ln_var = sem("ln_var")
        ln_rms = sem("ln_rms")
        ln_inverse = sem("ln_inverse")
        ln_spread = sem("ln_spread")
        ln_scaled = sem("ln_scaled")
        u_act = sem("u_act")
        u_hi = sem("u_hi")
        mix_split = sem("mix_split")
        mix_sq = sem("mix_sq")
        mix_scaled = sem("mix_scaled")
        x_new = sem("x_new")
        half_closed = sem("half_closed")
        crossed = sem("crossed")
        summed = sem("summed")
        silu_done = sem("silu_done")
        prod_done = sem("prod_done")
        hid_hi = sem("hid_hi")
        hid_lo = sem("hid_lo")
        f_sq = sem("f_sq")
        f_scaled = sem("f_scaled")
        out_made = sem("out_made")

        def pcol(name, i, n=1):
            return par[:, PAT[name] + i:PAT[name] + i + n]

        eps = stat[:, 0:1]
        ssq, rms, rstd = stat[:, 2:4], stat[:, 4:6], stat[:, 6:8]
        gn_inv_col, ln_inv_col = stat[:, 16:24], stat[:, 24:26]
        gn_rms_col, ln_rms_col = stat[:, 26:34], stat[:, 34:36]
        sq_part = stat[:, 8:16].rearrange("p (h c) -> p h c", c=NCH)

        def rows(w):
            return w.rearrange("(k p) n -> p k n", p=P)

        win_r, wout_r, gate_r, up_r, down_r = rows(w_in), rows(w_out), rows(w_gate), rows(w_up), rows(w_down)
        x_r = x.rearrange("(h p) d -> p h d", p=P)
        out_r = out.rearrange("(h p) d -> p h d", p=P)

        block = ctx.enter_context(nc.Block())

        @block.sync
        def _(sp):
            def load(q, i, k, src):
                if not (isinstance(q, int) and q == 0):
                    sp.wait_ge(lo_made, 4 * q + (i + 1 - SLOTS))
                sp.dma_start(raw[:, i, :].rearrange("p (k n) -> p k n", k=k), src).then_inc(unit_loaded[i], 16)

            def load_slab(q, w, col):
                for i in range(4):
                    load(q, i, 4, w[:, 4 * i:4 * i + 4, bass.ds(col, SLAB)])

            for h in range(TH):
                sp.dma_start(x_row[:, h, :], x_r[:, h, :]).then_inc(x_loaded[h], 16)
            load_slab(0, win_r, COL_GATE)
            sp.dma_start(dt_raw[:, :, :], win_r[:, :, COL_DT:COL_DT + HEADS]).then_inc(dtw_loaded, 16)
            load_slab(1, win_r, COL_A)
            sp.dma_start(post_g[:, :], post_mix.partition_broadcast(P)).then_inc(postg_loaded, 16)
            with sp.Fori(0, PAIRS - 1) as j:
                load_slab(2 * j + 2, win_r, SLAB * j + (COL_GATE + SLAB))
                load_slab(2 * j + 3, win_r, SLAB * j + (COL_A + SLAB))
            with sp.Fori(0, XBC_SLABS) as m:
                load_slab(m + SLAB_X, win_r, SLAB * m + COL_XBC)
            with sp.Fori(0, Z_SLABS) as m:
                load_slab(m + SLAB_Z, win_r, SLAB * m + COL_Z)
            for n, (c, kp) in enumerate(WOUT_ORDER):
                load(QUAD_WOUT + n // 4, n % 4, 2, wout_r[:, 2 * kp:2 * kp + 2, 512 * c:512 * c + 512])
            with sp.Fori(0, FFN_PAIRS) as j:
                load_slab(2 * j + QUAD_FFN, gate_r, SLAB * j)
                load_slab(2 * j + (QUAD_FFN + 1), up_r, SLAB * j)
            sp.wait_ge(mix_scaled, TH * NCH)
            sp.dma_start(post_g[:, :], post_ffn.partition_broadcast(P)).then_inc(postg_loaded, 16)
            with sp.Fori(0, NCH // 2) as cp:
                for n in range(2 * DOWN_UNITS):
                    k, c = n % DOWN_UNITS, n // DOWN_UNITS
                    load(DOWN_UNITS // 2 * cp + (QUAD_DOWN + n // 4), n % 4, 2,
                         down_r[:, 2 * k:2 * k + 2, bass.ds(1024 * cp + 512 * c, 512)])
            for h in range(TH):
                for c, part in enumerate(OUT_PARTS):
                    sp.wait_ge(out_made, len(OUT_PARTS) * h + c + 1)
                    sp.dma_start(out_r[:, h, part], f_row[:, h, part]).then_inc(stored, 16)
            sp.wait_ge(stored, 16 * len(OUT_PARTS) * TH)

        @block.gpsimd
        def _(pool):
            pool.memset(stat[:, 0:1], EPS).then_inc(eps_set, 1)
            pool.memset(ident[:, :], 0.0).then_inc(consts, 1)
            pool.memset(sel[:, :, :], 0.0).then_inc(consts, 1)
            pool.memset(mask[:, :], 1.0).then_inc(consts, 1)
            pool.memset(mean_w[:, :], 1.0 / DC).then_inc(consts, 1)
            pool.memset(upad[:, :, 0:TAPS - 1], 0.0).then_inc(consts, 1)
            pool.memset(xpad[:, :, :, 0:TAPS4 - 1], 0.0).then_inc(consts, 1)
            pool.memset(stat[:, 40:41], 0.0).then_inc(f_scaled, BANK_CREDIT)
            pool.wait_ge(consts, 6)
            pool.affine_select(out=ident[:, :], in_=ident[:, :], compare_op=ALU.not_equal, fill=1.0, base=0,
                               pattern=[[-1, P]], channel_multiplier=1).then_inc(consts, 1)
            pool.affine_select(out=sel[:, :, :], in_=sel[:, :, :], compare_op=ALU.not_equal, fill=1.0, base=0,
                               pattern=[[-1, HEADS], [0, P]], channel_multiplier=1).then_inc(consts, 1)
            pool.affine_select(out=mask[:, 0:T], in_=mask[:, 0:T], compare_op=ALU.is_ge, fill=0.0, base=0,
                               pattern=[[1, T]], channel_multiplier=-1).then_inc(consts, 1)
            pool.affine_select(out=mask[:, T:T + P], in_=mask[:, T:T + P], compare_op=ALU.is_ge, fill=0.0, base=0,
                               pattern=[[1, P]], channel_multiplier=-1).then_inc(consts, 1)
        CONSTS = 10

        @block.scalar
        def _(act):
            def hi(q, i):
                act.wait_ge(unit_loaded[i], 16 * q + 16)
                if not (isinstance(q, int) and q == 0):
                    act.wait_ge(multiplied, 4 * q + (i + 1 - SLOTS))
                act.activation(w_hi[:, i, :], raw[:, i, :], ACT.Copy).then_inc(hi_made, 1)

            def cross_copy(f, parity):
                act.wait_ge(multiplied, 4 * f + (4 * QUAD_FFN + 4))
                if not (isinstance(f, int) and f < 2):
                    act.wait_ge(summed, f - 1)
                b = 2 * parity
                act.activation(cross[:, parity, :, :], ps[:, b:b + 2, CROSS], ACT.Copy).then_inc(crossed, 1)

            def quad(q, before=None, f0=None):
                hi(q, 0)
                if f0:
                    f0()
                hi(q, 1)
                hi(q, 2)
                if before:
                    before()
                hi(q, 3)

            def warm_sqrt(n):
                if n:
                    act.wait_ge(warmed, n)
                act.activation(stat[:, 41:42], eps, ACT.Sqrt).then_inc(warmed, 1)

            def row_root(h):
                act.activation(rms[:, h:h + 1], ssq[:, h:h + 1], ACT.Sqrt, bias=eps, scale=1.0 / D).then_inc(row_rms, 1)

            def row_norm_start(n):
                for h in range(TH):
                    if n == 0:
                        act.wait_ge(x_loaded[h], 16)
                    else:
                        act.wait_ge(x_new, h + 1)
                    act.activation(row_work[:, h, :], x_row[:, h, :], ACT.Square,
                                   accum_out=ssq[:, h:h + 1]).then_inc(row_sq, 1)
                    act.wait_ge(row_sq, TH * n + h + 1)
                    row_root(h)

            def norm_split_hi(n, gain, unit=None):
                for kp in range(KC // 2):
                    if unit and kp % 2 == 0:
                        unit(kp // 2)
                    act.wait_ge(turned, n * (KC // 2) + kp + 1)
                    for k in range(2):
                        kc = 2 * kp + k
                        act.activation(acts[:, kc, 0, :], ps[:, 4 + kp % 4, k * T:k * T + T], ACT.Copy,
                                       scale=pcol(gain, kc)).then_inc(norm_hi, 1)

            act.dma_start(par[:, :], params).then_inc(par_loaded, 16)
            act.wait_ge(eps_set, 1)
            warm_sqrt(0)
            row_norm_start(0)
            act.wait_ge(par_loaded, 16)
            norm_split_hi(0, "mix_g", lambda i: hi(0, i))
            act.wait_ge(dtw_loaded, 16)
            act.activation(dt_w[:, :, 0, :], dt_raw[:, :, :], ACT.Copy).then_inc(dtw_hi_made, 1)

            def gate_sigmoid(j):
                act.wait_ge(multiplied, 8 * j + 4)
                if not isinstance(j, int):
                    act.wait_ge(glu_done, j)
                act.activation(gate_buf[:, :, :], ps[:, 0:2, MAIN], ACT.Sigmoid).then_inc(gate_sig, 1)

            def conv_start(j):
                act.wait_ge(glu_done, j + 1)
                for b in range(2):
                    act.activation(u[:, bass.ds(2 * j + b, 1), :], upad[:, bass.ds(2 * j + b, 1), 0:T], ACT.Identity,
                                   bias=par[:, bass.ds(2 * j + (b + PAT["dw_b"]), 1)],
                                   scale=par[:, bass.ds((2 * j + b) * TAPS + PAT["dw_w"], 1)]).then_inc(conv_first, 1)

            def x_start(m, parity):
                act.wait_ge(multiplied, 4 * m + (4 * SLAB_X + 4))
                for b in range(2):
                    act.activation(xbc[:, bass.ds(2 * m + b, 1), :], ps[:, 2 * parity + b:2 * parity + b + 1, MAIN], ACT.Identity,
                                   bias=par[:, bass.ds(2 * m + (b + PAT["xb"]), 1)],
                                   scale=par[:, bass.ds((2 * m + b) * TAPS4 + (PAT["xw"] + TAPS4 - 1), 1)]).then_inc(x_first, 1)
                act.activation(xpad[:, parity, :, TAPS4 - 1:XPW], ps[:, 2 * parity:2 * parity + 2, MAIN], ACT.Copy).then_inc(x_in, 1)

            def x_silu(m):
                act.wait_ge(x_tap, XOPS * m + XOPS)
                blocks = xbc_slabs[:, bass.ds(m, 1), :]
                act.activation(blocks, blocks, ACT.Silu).then_inc(x_act, 1)

            def z_silu(m):
                act.wait_ge(multiplied, 4 * (SLAB_Z + m) + 4)
                b = 2 * (m % 2)
                act.activation(z[:, 2 * m:2 * m + 2, :], ps[:, b:b + 2, MAIN], ACT.Silu).then_inc(z_act, 1)

            def relus(g):
                act.wait_ge(cs_spread, g + 1)
                for i in range(HPG):
                    h = HPG * g + i
                    row = ps[:, 4 + 2 * (g % 2) + i // 2, (i % 2) * T:(i % 2) * T + T]
                    act.activation(decay[:, g, i, 0:T], row, ACT.Relu, bias=cs_tab[:, h:h + 1], scale=-1.0).then_inc(relu_done, 1)
                    act.activation(decay[:, g, i, T:T + P], row[:, P:T], ACT.Relu, bias=cs_tab[:, HEADS + h:HEADS + h + 1],
                                   scale=-1.0).then_inc(relu_done, 1)

            def decays():
                act.wait_ge(relu_done, 2 * HEADS)
                for g in range(GROUPS):
                    act.activation(decay[:, g], decay[:, g], ACT.Exp, scale=-1.0).then_inc(decay_made, 1)

            xbc_slabs = xbc[:, :, :].rearrange("p (m b) t -> p m (b t)", b=2)
            quad(1, lambda: gate_sigmoid(0))
            act.wait_ge(dt_step, 2)
            act.activation(dt_e, dt_v, ACT.Abs).then_inc(dt_exp, 1)
            act.wait_ge(dt_exp, 1)
            act.activation(dt_e, dt_e, ACT.Exp, scale=-1.0).then_inc(dt_exp, 1)
            act.activation(a_exp[:, 0:HEADS], pcol("a_log", 0, HEADS), ACT.Exp).then_inc(dt_exp, 1)
            with act.Fori(1, PAIRS) as j:
                quad(2 * j)
                conv_start(j - 1)
                quad(2 * j + 1, lambda: gate_sigmoid(j))
            quad(SLAB_X)
            conv_start(PAIRS - 1)
            quad(SLAB_X + 1, lambda: x_start(0, 0))

            def x_pair(m, after0, after1):
                quad(2 * m + SLAB_X, lambda: x_start(2 * m - 1, 1), f0=lambda: x_silu(2 * m - 2))
                if after0:
                    after0()
                quad(2 * m + (SLAB_X + 1), lambda: x_start(2 * m, 0), f0=lambda: x_silu(2 * m - 1))
                if after1:
                    after1()

            with act.Fori(1, XBC_SLABS // 2 - 1) as m:
                x_pair(m, None, None)
            x_pair(XBC_SLABS // 2 - 1, lambda: relus(0), lambda: relus(1))
            quad(SLAB_Z, lambda: x_start(XBC_SLABS - 1, 1), f0=lambda: x_silu(XBC_SLABS - 2))
            relus(2)
            relus(3)
            quad(SLAB_Z + 1, lambda: z_silu(0), f0=lambda: x_silu(XBC_SLABS - 1))
            decays()
            quad(SLAB_Z + 2, lambda: z_silu(1))
            quad(SLAB_Z + 3, lambda: z_silu(2))

            def gated_squares(g):
                act.wait_ge(y_gated, g + 1)
                act.activation(z[:, 2 * g:2 * g + 2, :], xbc[:, 2 * g:2 * g + 2, :], ACT.Square).then_inc(y_sq, 1)

            def group_rms(gp):
                act.wait_ge(gn_stat, gp + 1)
                act.activation(gn_rms_col[:, 4 * gp:4 * gp + 4], ps[:, 4 + 2 * gp, 0:4], ACT.Sqrt, bias=eps,
                               scale=float(GROUPS)).then_inc(gn_rms, 1)

            def y_split_hi(gp):
                for m in range(4 * gp, 4 * gp + 4):
                    act.wait_ge(y_scaled, m // 2 + 1)
                    act.activation(acts[:, CB + m, 0, :], xbc[:, m, :], ACT.Copy, scale=pcol("gn_w", m)).then_inc(y_hi, 1)

            gated_squares(0)
            gated_squares(1)
            hi(QUAD_WOUT, 0)
            group_rms(0)
            hi(QUAD_WOUT, 1)
            hi(QUAD_WOUT, 2)
            act.wait_ge(multiplied, 4 * QUAD_WOUT)
            y_split_hi(0)
            z_silu(3)
            hi(QUAD_WOUT, 3)
            gated_squares(2)
            gated_squares(3)
            hi(QUAD_WOUT + 1, 0)
            group_rms(1)
            hi(QUAD_WOUT + 1, 1)
            y_split_hi(1)
            for n in range(6, AT_MEAN + 4):
                hi(QUAD_WOUT + n // 4, n % 4)
            act.wait_ge(ln_cent, 1)
            act.activation(upad[:, :, 0:T], u[:, :, :], ACT.Square).then_inc(ln_sq, 1)
            for n in range(AT_MEAN + 4, AT_VAR + 3):
                hi(QUAD_WOUT + n // 4, n % 4)
            act.wait_ge(ln_var, 1)
            act.activation(ln_rms_col, ps[:, 7, 0:TH], ACT.Sqrt, bias=eps).then_inc(ln_rms, 1)
            for n in range(AT_VAR + 3, U_UNIT + 1):
                hi(QUAD_WOUT + n // 4, n % 4)
            act.wait_ge(ln_scaled, 1)
            for b in range(CB):
                act.activation(u[:, b, :], u[:, b, :], ACT.Silu, bias=pcol("ln_b", b), scale=pcol("ln_g", b)).then_inc(u_act, 1)
                if b % 2:
                    act.wait_ge(u_act, b + 1)
                    act.activation(acts[:, b - 1:b + 1, 0, :], u[:, b - 1:b + 1, :], ACT.Copy).then_inc(u_hi, 1)
                    n = U_UNIT + 1 + b // 2
                    hi(QUAD_WOUT + n // 4, n % 4)

            def mix_square(c, h):
                act.activation(cross[:, h, :, :], ps[:, 2 * c + h, :], ACT.Square,
                               accum_out=sq_part[:, h, c:c + 1]).then_inc(mix_sq, 1)
                act.wait_ge(mix_sq, TH * c + h + 1)

            def f_square(c, h):
                act.activation(cross[:, h, :, :], ps[:, 4 + 2 * (c % 2) + h, :], ACT.Square,
                               accum_out=sq_part[:, h, c:c + 1]).then_inc(f_sq, 1)
                act.wait_ge(f_sq, TH * c + h + 1)

            def last_squares(square, n, units):
                for h in range(TH):
                    if h == 0:
                        act.wait_ge(half_closed, 1 + 2 * n)
                    else:
                        act.wait_ge(multiplied, units)
                    square(NCH - 1, h)
                    act.wait_ge(row_sum, TH * n + h + 1)
                    row_root(h)

            for n in range(U_UNIT + 1 + CB // 2, len(WOUT_ORDER)):
                hi(QUAD_WOUT + n // 4, n % 4)
                if n == len(WOUT_ORDER) - 5:
                    for c in range(NCH - 1):
                        act.wait_ge(multiplied, 4 * QUAD_WOUT + (LAST_OF_CHUNK[c] + 1))
                        for h in range(TH):
                            mix_square(c, h)
            hi(QUAD_FFN, 0)
            hi(QUAD_FFN, 1)
            hi(QUAD_FFN, 2)
            warm_sqrt(1)
            last_squares(mix_square, 0, 4 * QUAD_FFN)
            hi(QUAD_FFN, 3)
            row_norm_start(1)
            norm_split_hi(1, "ffn_g")

            def ffn_silu(j):
                act.wait_ge(summed, 2 * j + 1)
                act.activation(gate_buf[:, :, :], gate_buf[:, :, :], ACT.Silu).then_inc(silu_done, 1)

            def hidden_hi(j):
                act.wait_ge(prod_done, j + 1)
                act.activation(hidden[:, bass.ds(2 * j, 2), 0, :], up_buf[:, :, :], ACT.Copy).then_inc(hid_hi, 1)

            quad(QUAD_FFN + 1, lambda: cross_copy(0, 0))
            ffn_silu(0)
            with act.Fori(1, FFN_PAIRS) as j:
                quad(2 * j + QUAD_FFN, lambda: cross_copy(2 * j - 1, 1))
                hidden_hi(j - 1)
                quad(2 * j + (QUAD_FFN + 1), lambda: cross_copy(2 * j, 0))
                ffn_silu(j)
            hi(QUAD_DOWN, 0)
            hi(QUAD_DOWN, 1)
            hi(QUAD_DOWN, 2)
            cross_copy(2 * FFN_PAIRS - 1, 1)
            hidden_hi(FFN_PAIRS - 1)

            def f_squares(c):
                act.wait_ge(multiplied, 4 * QUAD_DOWN + DOWN_UNITS * (c + 1))
                for h in range(TH):
                    f_square(c, h)

            def down_hi(first, count):
                with act.Fori(0, count // 4) as g:
                    for n in range(first, first + 4):
                        hi(g + (QUAD_DOWN + n // 4), n % 4)
                for n in range(first + count // 4 * 4, first + count):
                    hi(QUAD_DOWN + n // 4, n % 4)

            down_hi(3, DOWN_UNITS)
            f_squares(0)
            down_hi(DOWN_UNITS + 3, DOWN_UNITS)
            f_squares(1)
            down_hi(2 * DOWN_UNITS + 3, DOWN_UNITS)
            f_squares(2)
            down_hi(3 * DOWN_UNITS + 3, DOWN_UNITS - 3)
            warm_sqrt(2)
            last_squares(f_square, 1, 4 * QUAD_DOWN + DOWN_UNITS * NCH)

        @block.vector
        def _(dve):
            def lo(q, i):
                dve.wait_ge(hi_made, 4 * q + (i + 1))
                dve.tensor_tensor(w_lo[:, i, :], raw[:, i, :], w_hi[:, i, :].bitcast(F32), ALU.subtract).then_inc(lo_made, 1)

            def sum_slab(f, parity, dst, free_sem=None, free_at=None):
                if free_sem is not None:
                    dve.wait_ge(free_sem, free_at)
                dve.wait_ge(crossed, f + 1)
                b = 2 * parity
                dve.tensor_tensor(dst, ps[:, b:b + 2, MAIN], cross[:, parity, :, :], ALU.add).then_inc(summed, 1)

            def quad(q, f0=None, f1=None, before=None, after=None):
                lo(q, 0)
                if f0:
                    f0()
                lo(q, 1)
                if f1:
                    f1()
                lo(q, 2)
                if before:
                    before()
                lo(q, 3)
                if after:
                    after()

            def row_inverse(stage, h):
                dve.wait_ge(row_rms, TH * stage + h + 1)
                dve.reciprocal(rstd[:, h:h + 1], rms[:, h:h + 1]).then_inc(row_rstd, 1)
                dve.wait_ge(row_rstd, TH * stage + h + 1)

            def row_sum_up(h):
                dve.tensor_reduce(ssq[:, h:h + 1], sq_part[:, h, :], mybir.AxisListType.X, ALU.add).then_inc(row_sum, 1)

            def row_norm_finish(n, between=None):
                if n == 0:
                    dve.wait_ge(consts, CONSTS)
                for h in range(TH):
                    if h == 1 and between:
                        between()
                    row_inverse(2 * n, h)
                    dve.tensor_scalar(diag[:, h, :], ident[:, :], rstd[:, h:h + 1], None, ALU.mult).then_inc(diag_made, 1)

            def norm_split_lo(n, gain, unit=None):
                for kp in range(KC // 2):
                    if unit and kp % 2 == 0:
                        unit(kp // 2)
                    dve.wait_ge(norm_hi, n * KC + 2 * kp + 2)
                    for k in range(2):
                        kc = 2 * kp + k
                        dve.scalar_tensor_tensor(acts[:, kc, 1, :], ps[:, 4 + kp % 4, k * T:k * T + T], pcol(gain, kc),
                                                 acts[:, kc, 0, :].bitcast(F32), ALU.mult, ALU.subtract).then_inc(norm_lo, 1)

            row_norm_finish(0)
            norm_split_lo(0, "mix_g", lambda i: lo(0, i))
            dve.wait_ge(dtw_hi_made, 1)
            dve.tensor_tensor(dt_w[:, :, 1, :], dt_raw[:, :, :], dt_w[:, :, 0, :].bitcast(F32), ALU.subtract).then_inc(dtw_lo_made, 1)

            def take_dt():
                dve.wait_ge(dt_done, 1)
                dve.tensor_copy(dt_row[:, :], ps[0:2 * HEADS, 4, :]).then_inc(dt_copied, 1)

            quad(1, f1=take_dt)

            dve.wait_ge(dt_turned, 1)
            for h in range(TH):
                dve.tensor_tensor(dt_v[:, h * HEADS:(h + 1) * HEADS], ps[:, 5, h * HEADS:(h + 1) * HEADS], pcol("dt_bias", 0, HEADS),
                                  ALU.add).then_inc(dt_step, 1)
            dve.wait_ge(dt_exp, 3)
            step = [TH]

            def small(ins):
                ins.then_inc(dt_step, 1)
                step[0] += 1
                dve.wait_ge(dt_step, step[0])

            small(dve.tensor_scalar(ser_s, dt_e, 2.0, None, ALU.add))
            small(dve.reciprocal(ser_q, ser_s))
            small(dve.tensor_tensor(ser_s, dt_e, ser_q, ALU.mult))
            small(dve.tensor_tensor(ser_q, ser_s, ser_s, ALU.mult))
            small(dve.tensor_scalar(ser_acc, ser_q, SERIES[-1], None, ALU.mult))
            for c in SERIES[-2:0:-1]:
                small(dve.scalar_tensor_tensor(ser_acc, ser_acc, c, ser_q, ALU.add, ALU.mult))
            small(dve.scalar_tensor_tensor(ser_acc, ser_acc, 1.0, ser_s, ALU.add, ALU.mult))
            small(dve.tensor_scalar(ser_s, dt_v, 0.0, None, ALU.max))
            small(dve.scalar_tensor_tensor(dt_tab, ser_acc, 2.0, ser_s, ALU.mult, ALU.add))
            for h in range(TH):
                dve.scalar_tensor_tensor(a_tab[:, h * HEADS:(h + 1) * HEADS], dt_tab[:, h * HEADS:(h + 1) * HEADS], -1.0,
                                         a_exp[:, 0:HEADS], ALU.mult, ALU.mult).then_inc(a_ready, 1)

            def glu(j):
                dve.wait_ge(gate_sig, j + 1)
                dve.wait_ge(multiplied, 8 * j + 8)
                dve.tensor_tensor(upad[:, bass.ds(2 * j, 2), TAPS - 1:PADW], ps[:, 2:4, MAIN], gate_buf[:, :, :],
                                  ALU.mult).then_inc(glu_done, 1)

            def conv(pair, k0, k1, seg, at):
                for k in range(k0, k1):
                    for b in range(2):
                        if k > seg:
                            dve.wait_ge(conv_tap, at + (2 * (k - 1 - seg) + b + 1))
                        elif k == 1:
                            dve.wait_ge(conv_first, 2 * pair + (b + 1))
                        else:
                            dve.wait_ge(conv_tap, at)
                        dst = u[:, bass.ds(2 * pair + b, 1), :]
                        dve.scalar_tensor_tensor(dst, upad[:, bass.ds(2 * pair + b, 1), k:k + T],
                                                 par[:, bass.ds((2 * pair + b) * TAPS + (PAT["dw_w"] + k), 1)], dst,
                                                 ALU.mult, ALU.add).then_inc(conv_tap, 1)

            def x_after(m, parity):
                dve.wait_ge(x_in, m + 1)
                for k in range(TAPS4 - 1):
                    for b in range(2):
                        if k == 0:
                            dve.wait_ge(x_first, 2 * m + (b + 1))
                        else:
                            dve.wait_ge(x_tap, XOPS * m + (2 * (k - 1) + b + 1))
                        dst = xbc[:, bass.ds(2 * m + b, 1), :]
                        dve.scalar_tensor_tensor(dst, xpad[:, parity, b:b + 1, k:k + T],
                                                 par[:, bass.ds((2 * m + b) * TAPS4 + (PAT["xw"] + k), 1)], dst,
                                                 ALU.mult, ALU.add).then_inc(x_tap, 1)

            def cuts(k0, k1, n):
                return [k0 + (k1 - k0) * i // n for i in range(n + 1)]

            first_taps = cuts(1, 1 + SEG_A, 4)
            later_taps = cuts(1 + SEG_A, TAPS, 7)

            def seg_a(m, i):
                conv(m, first_taps[i], first_taps[i + 1], 1, 2 * SEG_A * m)

            def seg_b(m, i, n=1):
                conv(m, later_taps[i], later_taps[i + n], 1 + SEG_A, 2 * SEG_B * m + AT_B)

            def a_quad(j):
                quad(2 * j + 1, f0=lambda: seg_a(j - 1, 0), f1=lambda: seg_a(j - 1, 1), after=lambda: seg_a(j - 1, 2))

            quad(2, before=lambda: glu(0))
            with dve.Fori(1, PAIRS - 1) as j:
                a_quad(j)
                quad(2 * j + 2, f0=lambda: seg_a(j - 1, 3), before=lambda: glu(j))
            a_quad(PAIRS - 1)
            quad(SLAB_X, f0=lambda: seg_a(PAIRS - 2, 3), f1=lambda: seg_b(0, 0, 2), before=lambda: glu(PAIRS - 1))
            dve.wait_ge(cs_done, 1)
            dve.tensor_copy(cs_tab, ps[:, 6, 0:2 * HEADS]).then_inc(cs_copied, 1)
            quad(SLAB_X + 1, f0=lambda: seg_b(0, 2, 3), f1=lambda: seg_b(0, 5, 2), after=lambda: x_after(0, 0))
            dve.wait_ge(csT_done, 1)
            dve.tensor_copy(cs_row[:, :], ps[0:HEADS, 7, 0:T]).then_inc(csT_copied, 1)

            def x_pair(m, run):
                quad(2 * m + SLAB_X, f0=lambda: run(0), f1=lambda: run(1), after=lambda: x_after(2 * m - 1, 1))
                quad(2 * m + (SLAB_X + 1), f0=lambda: run(2), f1=lambda: run(3), after=lambda: x_after(2 * m, 0))

            with dve.Fori(1, XBC_SLABS // 2 - 1) as m:
                x_pair(m, lambda i: seg_b(m, 2 * i, 1 if i == 3 else 2))
            third_taps = cuts(1, 1 + SEG_C, 4)
            x_pair(XBC_SLABS // 2 - 1, lambda i: conv(PAIRS - 1, third_taps[i], third_taps[i + 1], 1, AT_C))

            def decayed_scores(g):
                dve.wait_ge(decay_made, g + 1)
                dve.tensor_tensor(decay[:, g], decay[:, g],
                                  scores[:, g:g + 1, :].to_broadcast([P, HPG, T + P]), ALU.mult).then_inc(scores_decayed, 1)

            def skip(g):
                dve.wait_ge(y_done, g + 1)
                for b in range(2):
                    m = 2 * g + b
                    dve.scalar_tensor_tensor(xbc[:, m, :], xbc[:, m, :], pcol("d_skip", m), ps[:, 4 + g, b * T:(b + 1) * T],
                                             ALU.mult, ALU.add).then_inc(y_skip, 1)

            last_taps = cuts(1 + SEG_C, TAPS, 8)

            def seg_d(i):
                conv(PAIRS - 1, last_taps[i], last_taps[i + 1], 1 + SEG_C, AT_D)

            quad(SLAB_Z, f0=lambda: seg_d(0), f1=lambda: seg_d(1), after=lambda: x_after(XBC_SLABS - 1, 1))
            quad(SLAB_Z + 1, f0=lambda: seg_d(2), f1=lambda: seg_d(3))
            for n in range(4):
                h, mq = n // 2, n % 2
                dve.wait_ge(xs_turned, n + 1)
                dve.tensor_tensor(xd[:, h, mq * 512:(mq + 1) * 512].rearrange("p (e d) -> p e d", d=HD),
                                  ps[:, 4 + n, :].rearrange("p (e d) -> p e d", d=HD),
                                  dt_tab[:, h * HEADS + 8 * mq:h * HEADS + 8 * mq + 8].unsqueeze(2).to_broadcast([P, 8, HD]),
                                  ALU.mult).then_inc(xd_made, 1)
            quad(SLAB_Z + 2, f0=lambda: seg_d(4))
            for g in range(GROUPS):
                dve.wait_ge(scored, g + 1)
                dve.tensor_tensor(scores[:, g, :], ps[:, 4 + g, 0:T + P], mask[:, :], ALU.mult).then_inc(masked, 1)
            dve.wait_ge(masked, GROUPS)
            decayed_scores(0)
            decayed_scores(1)
            quad(SLAB_Z + 3, f0=lambda: decayed_scores(2), f1=lambda: decayed_scores(3))

            def gate(g):
                dve.wait_ge(z_act, g + 1)
                dve.wait_ge(y_skip, 2 * g + 2)
                dve.tensor_tensor(xbc[:, 2 * g:2 * g + 2, :], xbc[:, 2 * g:2 * g + 2, :], z[:, 2 * g:2 * g + 2, :],
                                  ALU.mult).then_inc(y_gated, 1)

            def group_scale(gp):
                for g in (2 * gp, 2 * gp + 1):
                    dve.wait_ge(gn_spread, gp + 1)
                    dve.tensor_tensor(xbc[:, 2 * g:2 * g + 2, :], xbc[:, 2 * g:2 * g + 2, :],
                                      ps[:, 5 + 2 * gp:6 + 2 * gp, (g % 2) * T:(g % 2) * T + T].to_broadcast([P, 2, T]),
                                      ALU.mult).then_inc(y_scaled, 1)

            def group_inverse(gp):
                dve.wait_ge(gn_rms, gp + 1)
                dve.reciprocal(gn_inv_col[:, 4 * gp:4 * gp + 4], gn_rms_col[:, 4 * gp:4 * gp + 4]).then_inc(gn_inverse, 1)

            def y_split_lo(gp):
                for m in range(4 * gp, 4 * gp + 4):
                    dve.wait_ge(y_hi, m + 1)
                    dve.scalar_tensor_tensor(acts[:, CB + m, 1, :], xbc[:, m, :], pcol("gn_w", m),
                                             acts[:, CB + m, 0, :].bitcast(F32), ALU.mult, ALU.subtract).then_inc(mix_split, 1)

            skip(0)
            skip(1)
            gate(0)
            gate(1)
            lo(QUAD_WOUT, 0)
            group_inverse(0)
            skip(2)
            skip(3)
            gate(2)
            lo(QUAD_WOUT, 1)
            group_scale(0)
            lo(QUAD_WOUT, 2)
            y_split_lo(0)
            gate(3)
            lo(QUAD_WOUT, 3)
            seg_d(5)
            seg_d(6)
            seg_d(7)
            group_inverse(1)
            lo(QUAD_WOUT + 1, 0)
            group_scale(1)
            lo(QUAD_WOUT + 1, 1)
            y_split_lo(1)
            lo(QUAD_WOUT + 1, 2)
            for n in range(7, AT_MEAN + 4):
                lo(QUAD_WOUT + n // 4, n % 4)
            dve.wait_ge(ln_mean, 1)
            dve.tensor_tensor(u[:, :, :], u[:, :, :], ps[:, 6:7, 0:T].to_broadcast([P, CB, T]), ALU.subtract).then_inc(ln_cent, 1)
            for n in range(AT_MEAN + 4, AT_VAR + 3):
                lo(QUAD_WOUT + n // 4, n % 4)
            dve.wait_ge(ln_rms, 1)
            dve.reciprocal(ln_inv_col, ln_rms_col).then_inc(ln_inverse, 1)
            for n in range(AT_VAR + 3, U_UNIT + 1):
                lo(QUAD_WOUT + n // 4, n % 4)
            dve.wait_ge(ln_spread, 1)
            dve.wait_ge(ln_sq, 1)
            dve.tensor_tensor(u[:, :, :], u[:, :, :], ps[:, 7:8, T:2 * T].to_broadcast([P, CB, T]), ALU.mult).then_inc(ln_scaled, 1)
            for b in range(0, CB, 2):
                dve.wait_ge(u_hi, b // 2 + 1)
                dve.tensor_tensor(acts[:, b:b + 2, 1, :], u[:, b:b + 2, :], acts[:, b:b + 2, 0, :].bitcast(F32),
                                  ALU.subtract).then_inc(mix_split, 1)
                n = U_UNIT + 1 + b // 2
                lo(QUAD_WOUT + n // 4, n % 4)

            def scale_rows(c, h):
                dve.wait_ge(mix_sq, TH * c + h + 1)
                dve.tensor_tensor(row_work[:, h, 512 * c:512 * c + 512], ps[:, 2 * c + h, :],
                                  post_g[:, 512 * c:512 * c + 512], ALU.mult).then_inc(mix_scaled, 1)

            for n in range(U_UNIT + 1 + CB // 2, len(WOUT_ORDER)):
                lo(QUAD_WOUT + n // 4, n % 4)
                if n == len(WOUT_ORDER) - 5:
                    dve.wait_ge(postg_loaded, 16)
                    for c in range(NCH - 1):
                        for h in range(TH):
                            scale_rows(c, h)
            lo(QUAD_FFN, 0)
            lo(QUAD_FFN, 1)
            lo(QUAD_FFN, 2)
            for h in range(TH):
                dve.wait_ge(mix_sq, TH * (NCH - 1) + h + 1)
                row_sum_up(h)
                scale_rows(NCH - 1, h)
                row_inverse(1, h)
                dve.wait_ge(mix_scaled, TH * (NCH - 1) + h + 1)
                dve.scalar_tensor_tensor(x_row[:, h, :], row_work[:, h, :], rstd[:, h:h + 1], x_row[:, h, :],
                                         ALU.mult, ALU.add).then_inc(x_new, 1)
            row_norm_finish(1, between=lambda: lo(QUAD_FFN, 3))
            norm_split_lo(1, "ffn_g")

            def product(j):
                dve.wait_ge(silu_done, j + 1)
                dve.wait_ge(summed, 2 * j + 2)
                dve.tensor_tensor(up_buf[:, :, :], up_buf[:, :, :], gate_buf[:, :, :], ALU.mult).then_inc(prod_done, 1)

            def hidden_lo(j):
                dve.wait_ge(hid_hi, j + 1)
                dve.tensor_tensor(hidden[:, bass.ds(2 * j, 2), 1, :], up_buf[:, :, :],
                                  hidden[:, bass.ds(2 * j, 2), 0, :].bitcast(F32), ALU.subtract).then_inc(hid_lo, 1)

            def up_epilogue(j):
                if isinstance(j, int) and j == 0:
                    sum_slab(1, 1, up_buf[:, :, :])
                else:
                    sum_slab(2 * j + 1, 1, up_buf[:, :, :], hid_lo, j)
                product(j)

            quad(QUAD_FFN + 1, before=lambda: sum_slab(0, 0, gate_buf[:, :, :]))

            def ffn_pair(j):
                quad(2 * j + QUAD_FFN, before=lambda: up_epilogue(j - 1), after=lambda: hidden_lo(j - 1))
                quad(2 * j + (QUAD_FFN + 1), before=lambda: sum_slab(2 * j, 0, gate_buf[:, :, :], prod_done, j))

            ffn_pair(1)
            with dve.Fori(2, FFN_PAIRS) as j:
                ffn_pair(j)
            lo(QUAD_DOWN, 0)
            lo(QUAD_DOWN, 1)
            lo(QUAD_DOWN, 2)
            up_epilogue(FFN_PAIRS - 1)
            hidden_lo(FFN_PAIRS - 1)

            def scale_f(c, halves=range(TH)):
                for h in halves:
                    dve.wait_ge(f_sq, TH * c + h + 1)
                    dve.tensor_tensor(f_row[:, h, 512 * c:512 * c + 512], ps[:, 4 + 2 * (c % 2) + h, :],
                                      post_g[:, 512 * c:512 * c + 512], ALU.mult).then_inc(f_scaled, 1)

            def down_lo(first, count):
                with dve.Fori(0, count // 4) as g:
                    for n in range(first, first + 4):
                        lo(g + (QUAD_DOWN + n // 4), n % 4)
                for n in range(first + count // 4 * 4, first + count):
                    lo(QUAD_DOWN + n // 4, n % 4)

            down_lo(3, DOWN_UNITS)
            dve.wait_ge(postg_loaded, 32)
            scale_f(0)
            down_lo(DOWN_UNITS + 3, DOWN_UNITS)
            scale_f(1)
            down_lo(2 * DOWN_UNITS + 3, DOWN_UNITS)
            scale_f(2)
            down_lo(3 * DOWN_UNITS + 3, DOWN_UNITS - 3)
            for h in range(TH):
                dve.wait_ge(f_sq, TH * (NCH - 1) + h + 1)
                row_sum_up(h)
                scale_f(NCH - 1, [h])
                row_inverse(3, h)
                dve.wait_ge(f_scaled, BANK_CREDIT + TH * (NCH - 1) + h + 1)
                for part in OUT_PARTS:
                    dve.scalar_tensor_tensor(f_row[:, h, part], f_row[:, h, part], rstd[:, h:h + 1], x_row[:, h, part],
                                             ALU.mult, ALU.add).then_inc(out_made, 1)

        @block.tensor
        def _(pe):
            def slab(q, parity, free=None, joined=False, between=None):
                if free:
                    pe.wait_ge(*free)
                b0 = 2 * parity
                for i in range(4):
                    if between:
                        between(i)
                    pe.wait_ge(lo_made, 4 * q + (i + 1))
                    hi_t = w_hi[:, i, :].rearrange("p (k n) -> p k n", k=4)
                    lo_t = w_lo[:, i, :].rearrange("p (k n) -> p k n", k=4)
                    for b in range(2):
                        for k in range(4):
                            kc = 4 * i + k
                            if joined:
                                pe.matmul(ps[:, b0 + b, MAIN], hi_t[:, k, b * P:(b + 1) * P], acts[:, kc, 0, :],
                                          start=(kc == 0), stop=False)
                                pe.matmul(ps[:, b0 + b, MAIN], hi_t[:, k, b * P:(b + 1) * P], acts[:, kc, 1, :],
                                          start=False, stop=False)
                            else:
                                pe.matmul(ps[:, b0 + b, :], hi_t[:, k, b * P:(b + 1) * P],
                                          acts[:, kc, :, :].rearrange("p a t -> p (a t)"), start=(kc == 0), stop=False)
                            last = pe.matmul(ps[:, b0 + b, MAIN], lo_t[:, k, b * P:(b + 1) * P], acts[:, kc, 0, :],
                                             start=False, stop=(kc == KC - 1))
                    last.then_inc(multiplied, 1)

            def turn_rows(n, k0, k1):
                for h in range(TH):
                    if k0 == 0:
                        pe.wait_ge(diag_made, TH * n + h + 1)
                    for kp in range(k0, k1):
                        if kp >= 4 and h == 0:
                            pe.wait_ge(norm_lo, n * KC + 2 * (kp - 4) + 2)
                        for k in range(2):
                            kc = 2 * kp + k
                            last = pe.matmul(ps[:, 4 + kp % 4, k * T + h * P:k * T + h * P + P],
                                             x_row[:, h, kc * P:(kc + 1) * P], diag[:, h, :], start=True, stop=True)
                        if h == TH - 1:
                            last.then_inc(turned, 1)

            def first_slab(n, q, joined):
                def ready(i):
                    if i in (1, 2):
                        turn_rows(n, 2 * i + 2, 2 * i + 4)
                    pe.wait_ge(norm_lo, n * KC + 4 * i + 4)
                turn_rows(n, 0, 3)
                turn_rows(n, 3, 4)
                slab(q, 0, None, joined, ready)

            def gate_slab(j):
                slab(2 * j, 0, (gate_sig, j), joined=True)

            def a_slab(j):
                slab(2 * j + 1, 1, (glu_done, j), joined=True)

            def x_slab(m, parity, free):
                slab(m + SLAB_X, parity, free, joined=True)

            first_slab(0, 0, True)
            pe.wait_ge(dtw_lo_made, 1)
            for kc in range(KC):
                last = pe.matmul(ps[0:2 * HEADS, 4, :], dt_w[:, kc, :, :].rearrange("p a n -> p (a n)"),
                                 acts[:, kc, :, :].rearrange("p a t -> p (a t)"), start=(kc == 0), stop=(kc == KC - 1))
            last.then_inc(dt_done, 1)

            def turn_dt(i):
                if i != 1:
                    return
                pe.wait_ge(dt_copied, 1)
                pick_hi, pick_lo = ident[0:2 * HEADS, 0:HEADS], ident[0:2 * HEADS, HEADS:2 * HEADS]
                for h in range(TH):
                    o = ps[:, 5, h * HEADS:(h + 1) * HEADS]
                    at = h * P
                    pe.matmul(o, dt_row[:, at:at + P], pick_hi, start=True, stop=False)
                    pe.matmul(o, dt_row[:, at:at + P], pick_lo, start=False, stop=False)
                    last = pe.matmul(o, dt_row[:, T + at:T + at + P], pick_hi, start=False, stop=True)
                last.then_inc(dt_turned, 1)

            slab(1, 1, joined=True, between=turn_dt)
            with pe.Fori(1, PAIRS) as j:
                gate_slab(j)
                a_slab(j)
            pe.wait_ge(a_ready, TH)
            pe.matmul(ps[:, 6, 0:HEADS], mask[:, 0:P], a_tab[:, 0:HEADS], start=True, stop=True)
            pe.matmul(ps[:, 6, HEADS:2 * HEADS], mask[:, P:T], a_tab[:, 0:HEADS], start=True, stop=False)
            pe.matmul(ps[:, 6, HEADS:2 * HEADS], mask[:, 0:P], a_tab[:, HEADS:2 * HEADS], start=False, stop=True).then_inc(cs_done, 1)
            x_slab(0, 0, (gate_sig, PAIRS))
            pe.wait_ge(cs_copied, 1)
            for h in range(TH):
                last = pe.transpose(ps[0:HEADS, 7, h * P:(h + 1) * P], cs_tab[:, h * HEADS:(h + 1) * HEADS], ident[:, :])
            last.then_inc(csT_done, 1)
            x_slab(1, 1, (glu_done, PAIRS))
            with pe.Fori(1, XBC_SLABS // 2 - 1) as m:
                x_slab(2 * m, 0, (x_in, 2 * m - 1))
                x_slab(2 * m + 1, 1, (x_in, 2 * m))

            def spread_cs(g):
                for i in range(HPG):
                    last = pe.matmul(ps[:, 4 + 2 * (g % 2) + i // 2, (i % 2) * T:(i % 2) * T + T], sel[:, HPG * g + i, :], cs_row[:, :],
                                     start=True, stop=True)
                last.then_inc(cs_spread, 1)

            def y_group(g):
                pe.wait_ge(scores_decayed, g + 1)
                for i in range(HPG):
                    h = HPG * g + i
                    o = ps[(i % 2) * HD:(i % 2) * HD + HD, 4 + g, (i // 2) * T:(i // 2) * T + T]
                    pe.matmul(o, xd[:, 0, h * HD:(h + 1) * HD], decay[:, g, i, 0:T], start=True, stop=False)
                    last = pe.matmul(o[:, P:T], xd[:, 1, h * HD:(h + 1) * HD], decay[:, g, i, T:T + P],
                                     start=False, stop=True)
                last.then_inc(y_done, 1)

            pe.wait_ge(csT_copied, 1)
            spread_cs(0)
            spread_cs(1)
            x_slab(XBC_SLABS - 2, 0, (x_in, XBC_SLABS - 3))
            pe.wait_ge(relu_done, 2 * HPG)
            spread_cs(2)
            x_slab(XBC_SLABS - 1, 1, (x_in, XBC_SLABS - 2))
            pe.wait_ge(relu_done, 2 * 2 * HPG)
            spread_cs(3)
            slab(SLAB_Z, 0, (x_in, XBC_SLABS - 1), joined=True)
            pe.wait_ge(x_act, XBC_SLABS)
            pe.wait_ge(relu_done, 2 * HEADS)
            for n in range(4):
                h, mq = n // 2, n % 2
                for i in range(4):
                    last = pe.transpose(ps[:, 4 + n, i * P:(i + 1) * P], xbc[:, 4 * mq + i, h * P:(h + 1) * P], ident[:, :])
                last.then_inc(xs_turned, 1)
            slab(SLAB_Z + 1, 1, (x_in, XBC_SLABS), joined=True)
            pe.wait_ge(xd_made, 4)
            for g in range(GROUPS):
                b, c = SB + g, SB + GROUPS + g
                pe.matmul(ps[:, 4 + g, 0:T], xbc[:, b, 0:P], xbc[:, c, :], start=True, stop=True)
                pe.matmul(ps[:, 4 + g, T:T + P], xbc[:, b, P:T], xbc[:, c, P:T], start=True, stop=True).then_inc(scored, 1)
            slab(SLAB_Z + 2, 0, (z_act, 1), joined=True)
            y_group(0)
            y_group(1)

            def group_stat(gp):
                pe.wait_ge(y_sq, 2 * gp + 2)
                for g in (2 * gp, 2 * gp + 1):
                    for h in range(TH):
                        n = TH * (g % 2) + h
                        for b in range(2):
                            last = pe.matmul(ps[:, 4 + 2 * gp, n:n + 1], z[:, 2 * g + b, h * P:(h + 1) * P],
                                             mean_w[:, 0:1], start=(b == 0), stop=(b == 1))
                last.then_inc(gn_stat, 1)

            def spread(dst, col):
                return pe.matmul(dst, col.to_broadcast([P, P]), ident[:, :], start=True, stop=True)

            def group_spread(gp):
                pe.wait_ge(gn_inverse, gp + 1)
                for g in (2 * gp, 2 * gp + 1):
                    for h in range(TH):
                        o = (g % 2) * T + h * P
                        last = spread(ps[:, 5 + 2 * gp, o:o + P], gn_inv_col[:, TH * g + h:TH * g + h + 1])
                last.then_inc(gn_spread, 1)

            def group_steps(i):
                if i == 1:
                    group_stat(0)
                if i == 2:
                    y_group(2)
                    y_group(3)
                    group_spread(0)

            slab(SLAB_Z + 3, 1, (z_act, 2), joined=True, between=group_steps)

            def ln_mean_step():
                pe.wait_ge(conv_tap, CONV_OPS)
                for b in range(CB):
                    last = pe.matmul(ps[:, 6, 0:T], mean_w[:, :], u[:, b, :], start=(b == 0), stop=(b == CB - 1))
                last.then_inc(ln_mean, 1)

            def ln_var_step():
                pe.wait_ge(ln_sq, 1)
                pe.wait_ge(y_scaled, GROUPS)
                for h in range(TH):
                    for b in range(CB):
                        last = pe.matmul(ps[:, 7, h:h + 1], upad[:, b, h * P:(h + 1) * P], mean_w[:, 0:1],
                                         start=(b == 0), stop=(b == CB - 1))
                last.then_inc(ln_var, 1)

            def ln_spread_step():
                pe.wait_ge(ln_inverse, 1)
                for h in range(TH):
                    last = spread(ps[:, 7, T + h * P:T + h * P + P], ln_inv_col[:, h:h + 1])
                last.then_inc(ln_spread, 1)

            def unit_order(last):
                return [(0, 0), (1, 0), (0, 1), (1, 1)] if last else [(0, 0), (0, 1), (1, 0), (1, 1)]

            for n, (c, kp) in enumerate(WOUT_ORDER):
                if n < 2:
                    pe.wait_ge(z_act, Z_SLABS - 1 + n)
                if n == 2:
                    pe.wait_ge(y_scaled, 2)
                    group_stat(1)
                if n == 3:
                    group_spread(1)
                if n == AT_MEAN:
                    ln_mean_step()
                if n == AT_VAR:
                    ln_var_step()
                if n == AT_SPREAD:
                    ln_spread_step()
                if c == 0 and kp >= CB // 2:
                    pe.wait_ge(mix_split, 2 * (kp - CB // 2) + 2)
                if c == 0 and kp < CB // 2:
                    pe.wait_ge(mix_split, SB + kp + 1)
                if n == 24:
                    pe.wait_ge(ln_scaled, 1)
                pe.wait_ge(lo_made, 4 * QUAD_WOUT + n + 1)
                first = c == NCH - 1 and kp == 0 or c < NCH - 1 and kp == CB // 2
                last_k = c == NCH - 1 and kp == KC // 2 - 1 or c < NCH - 1 and kp == CB // 2 - 1
                for k, h in unit_order(n == len(WOUT_ORDER) - 1):
                    o = ps[:, 2 * c + h, :]
                    xh = acts[:, 2 * kp + k, 0, h * P:(h + 1) * P]
                    xl = acts[:, 2 * kp + k, 1, h * P:(h + 1) * P]
                    wh = w_hi[:, n % 4, k * 512:(k + 1) * 512]
                    wl = w_lo[:, n % 4, k * 512:(k + 1) * 512]
                    pe.matmul(o, xh, wh, start=(first and k == 0), stop=False)
                    pe.matmul(o, xh, wl, start=False, stop=False)
                    last = pe.matmul(o, xl, wh, start=False, stop=(last_k and k == 1))
                    if n == len(WOUT_ORDER) - 1 and (k, h) == (1, 0):
                        last.then_inc(half_closed, 1)
                last.then_inc(multiplied, 1)

            pe.wait_ge(mix_scaled, TH * NCH)
            first_slab(1, QUAD_FFN, False)
            slab(QUAD_FFN + 1, 1)
            with pe.Fori(1, FFN_PAIRS) as j:
                slab(2 * j + QUAD_FFN, 0, (summed, 2 * j - 1))
                slab(2 * j + (QUAD_FFN + 1), 1, (summed, 2 * j))

            with pe.Fori(0, NCH // 2) as cp:
                for n in range(2 * DOWN_UNITS):
                    kp, c = n % DOWN_UNITS, n // DOWN_UNITS
                    if kp == 0:
                        pe.wait_ge(f_scaled, 4 * cp + (2 * c + 1))
                        pe.wait_ge(hid_lo, FFN_PAIRS - 1)
                    if kp == DOWN_UNITS - 1:
                        pe.wait_ge(hid_lo, FFN_PAIRS)
                    pe.wait_ge(lo_made, 2 * DOWN_UNITS * cp + (4 * QUAD_DOWN + n + 1))
                    for k, h in unit_order(n == 2 * DOWN_UNITS - 1):
                        o = ps[:, 4 + 2 * c + h, :]
                        xh = hidden[:, 2 * kp + k, 0, h * P:(h + 1) * P]
                        xl = hidden[:, 2 * kp + k, 1, h * P:(h + 1) * P]
                        wh = w_hi[:, n % 4, k * 512:(k + 1) * 512]
                        wl = w_lo[:, n % 4, k * 512:(k + 1) * 512]
                        pe.matmul(o, xh, wh, start=(kp == 0 and k == 0), stop=False)
                        pe.matmul(o, xh, wl, start=False, stop=False)
                        last = pe.matmul(o, xl, wh, start=False, stop=(kp == DOWN_UNITS - 1 and k == 1))
                        if n == 2 * DOWN_UNITS - 1 and (k, h) == (1, 0):
                            last.then_inc(half_closed, 1)
                    last.then_inc(multiplied, 1)


WOUT_ORDER = [(c, kp) for kp in list(range(CB // 2, KC // 2)) + list(range(CB // 2)) for c in range(NCH - 1)] + \
             [(NCH - 1, kp) for kp in range(KC // 2)]
LAST_OF_CHUNK = [max(n for n, (c, _) in enumerate(WOUT_ORDER) if c == chunk) for chunk in range(NCH)]


def kernel(**inputs):
    import numpy as np
    import concourse.bacc as bacc
    from concourse import mybir as _mybir
    from concourse.bass_utils import run_bass_kernel_spmd

    a = {n: np.ascontiguousarray(v) for n, v in inputs.items()}

    def chan(v):
        v = v.reshape(v.shape[0], -1)
        return v.reshape(v.shape[0] // P, P, -1).transpose(1, 0, 2).reshape(P, -1)

    cols = {
        "mix_g": chan(a["norm_mix_pre"][0]), "ffn_g": chan(a["norm_ffn_pre"][0]),
        "dw_w": chan(a["conv_dw_w"][0].T), "dw_b": chan(a["conv_dw_b"][0]),
        "ln_g": chan(a["conv_ln_g"][0]), "ln_b": chan(a["conv_ln_b"][0]),
        "xw": chan(a["ssd_conv_w"][0].T), "xb": chan(a["ssd_conv_b"][0]),
        "d_skip": chan(np.repeat(a["ssd_d"][0], HD)), "gn_w": chan(a["ssd_norm_w"][0]),
        "dt_bias": np.broadcast_to(a["ssd_dt_bias"][0], (P, HEADS)),
        "a_log": np.broadcast_to(a["ssd_a_log"][0], (P, HEADS)),
    }
    arrays = {
        "x": a["x"][0], "w_in": a["w_in"][0], "w_out": a["w_out"][0], "w_gate": a["w_gate"][0],
        "w_up": a["w_up"][0], "w_down": a["w_down"][0],
        "params": np.concatenate([cols[n] for n, _ in PCOLS], axis=1),
        "post_mix": a["norm_mix_post"][0], "post_ffn": a["norm_ffn_post"][0],
    }
    arrays = {"in_" + n: np.ascontiguousarray(v) for n, v in arrays.items()}
    nc = bacc.Bacc("TRN2", target_bir_lowering=False, num_devices=1)
    args = [nc.dram_tensor(n, v.shape, _mybir.dt.from_np(v.dtype), kind="ExternalInput").ap() for n, v in arrays.items()]
    out = nc.dram_tensor("out_x", (T, D), F32, kind="ExternalOutput").ap()
    build(nc, *args, out)
    r = run_bass_kernel_spmd(nc, [arrays], core_ids=[0])
    return r.results[0]["out_x"].reshape(1, T, D)
```
